# Optimizing a Trainium2 kernel written in Bass

```python
import math
import jax, jax.numpy as jnp
from jax import lax
import numpy as np

D_MODEL = 1024
BATCH = 1
SEQ = 512
DEPTH = 2
DEC_BATCH = 8
DEC_SEQ = 4
PAST_LEN = 4096
PAGE_SIZE = 128

D_MIX = D_MODEL
GROUP_WIDTH = D_MIX // 4
HEAD_DIM = 64
CONV_WIDTH = 4
EPS = 1e-6

SSD_WIDTH = GROUP_WIDTH
SSD_HEADS = SSD_WIDTH // HEAD_DIM
SSD_STATE = 64
SSD_GROUPS = 2
SSD_CONV_DIM = SSD_WIDTH + 2 * SSD_GROUPS * SSD_STATE
SSD_CHUNK = 64

RET_WIDTH = GROUP_WIDTH
RET_HEADS = RET_WIDTH // HEAD_DIM
RET_CHUNK = 64
ROPE_BASE = 10000.0

GLA_WIDTH = GROUP_WIDTH
GLA_HEADS = 4
GLA_KEY_WIDTH = GLA_WIDTH // 2
GLA_DK = GLA_KEY_WIDTH // GLA_HEADS
GLA_DV = GLA_WIDTH // GLA_HEADS
GLA_GATE_RANK = 16
GLA_GATE_TEMP = 16.0
GLA_CHUNK = 16

LRU_WIDTH = GROUP_WIDTH
LRU_BLOCKS = LRU_WIDTH // HEAD_DIM
LRU_BLOCK_DIM = HEAD_DIM
LRU_C = 8.0

D_FF = -(-8 * D_MODEL // (3 * 256)) * 256

IN_WIDTHS = (SSD_WIDTH, SSD_CONV_DIM, SSD_HEADS,
             RET_WIDTH, RET_WIDTH, RET_WIDTH, RET_WIDTH,
             GLA_KEY_WIDTH, GLA_KEY_WIDTH, GLA_WIDTH, GLA_GATE_RANK, GLA_WIDTH,
             LRU_WIDTH, LRU_WIDTH)
IN_DIM = sum(IN_WIDTHS)

kernel_name = 'hybrid_parallel_heads_decode_step'

def _chunk_len(l, chunk):
    return chunk if l % chunk == 0 else math.gcd(l, chunk)

def _split_points():
    return np.cumsum(np.array(IN_WIDTHS))[:-1].tolist()

def rms_norm(x, w):
    xf = x.astype(jnp.float32)
    y = xf * lax.rsqrt(jnp.mean(xf * xf, axis=-1, keepdims=True) + EPS)
    return (y * w.astype(jnp.float32)).astype(x.dtype)

def causal_conv(x, buf, w, b):
    xp = jnp.concatenate([buf.astype(x.dtype), x], axis=1)
    l = x.shape[1]
    y = sum(xp[:, j:j + l] * w[j] for j in range(CONV_WIDTH)) + b
    return y.astype(x.dtype), xp[:, -(CONV_WIDTH - 1):]

def rotary(x, pos):
    half = HEAD_DIM // 2
    inv = ROPE_BASE ** (-jnp.arange(half, dtype=jnp.float32) / half)
    ang = pos.astype(jnp.float32)[:, None] * inv[None, :]
    cos = jnp.cos(ang)[None, :, None, :]
    sin = jnp.sin(ang)[None, :, None, :]
    x1, x2 = x[..., :half], x[..., half:]
    return jnp.concatenate([x1 * cos - x2 * sin, x1 * sin + x2 * cos], axis=-1)

def chunk_scalar_decay(q, k, v, log_a, s0, chunk):
    b, l, h, dk = q.shape
    dv = v.shape[-1]
    c = _chunk_len(l, chunk)
    n = l // c
    f32 = jnp.float32
    qc = q.astype(f32).reshape(b, n, c, h, dk)
    kc = k.astype(f32).reshape(b, n, c, h, dk)
    vc = v.astype(f32).reshape(b, n, c, h, dv)
    cum = jnp.cumsum(log_a.astype(f32).reshape(b, n, c, h), axis=2)
    causal = jnp.tril(jnp.ones((c, c), dtype=bool))[None, None, :, :, None]
    decay = jnp.exp(jnp.where(causal, cum[:, :, :, None, :] - cum[:, :, None, :, :], -jnp.inf))
    scores = jnp.einsum('bnihd,bnjhd->bnijh', qc, kc) * decay
    o_intra = jnp.einsum('bnijh,bnjhv->bnihv', scores, vc)
    last = cum[:, :, -1]
    ds = jnp.einsum('bnjh,bnjhd,bnjhv->bnhdv', jnp.exp(last[:, :, None] - cum), kc, vc)

    def step(s, inp):
        ds_c, last_c = inp
        return jnp.exp(last_c)[..., None, None] * s + ds_c, s

    s_fin, s_enter = lax.scan(step, s0.astype(f32), (jnp.swapaxes(ds, 0, 1), jnp.swapaxes(last, 0, 1)))
    o_inter = jnp.einsum('bnihd,nbhdv->bnihv', qc * jnp.exp(cum)[..., None], s_enter)
    o = (o_intra + o_inter).reshape(b, l, h, dv)
    return o.astype(q.dtype), s_fin

def chunk_vector_decay(q, k, v, log_g, s0, chunk):
    b, l, h, dk = q.shape
    dv = v.shape[-1]
    c = _chunk_len(l, chunk)
    n = l // c
    f32 = jnp.float32
    qc = q.astype(f32).reshape(b, n, c, h, dk)
    kc = k.astype(f32).reshape(b, n, c, h, dk)
    vc = v.astype(f32).reshape(b, n, c, h, dv)
    cum = jnp.cumsum(log_g.astype(f32).reshape(b, n, c, h, dk), axis=2)
    causal = jnp.tril(jnp.ones((c, c), dtype=bool))[None, None, :, :, None, None]
    decay = jnp.exp(jnp.where(causal, cum[:, :, :, None] - cum[:, :, None, :], -jnp.inf))
    scores = jnp.einsum('bnihd,bnjhd,bnijhd->bnijh', qc, kc, decay)
    o_intra = jnp.einsum('bnijh,bnjhv->bnihv', scores, vc)
    last = cum[:, :, -1]
    ds = jnp.einsum('bnjhd,bnjhv->bnhdv', kc * jnp.exp(last[:, :, None] - cum), vc)

    def step(s, inp):
        ds_c, last_c = inp
        return jnp.exp(last_c)[..., None] * s + ds_c, s

    s_fin, s_enter = lax.scan(step, s0.astype(f32), (jnp.swapaxes(ds, 0, 1), jnp.swapaxes(last, 0, 1)))
    o_inter = jnp.einsum('bnihd,nbhdv->bnihv', qc * jnp.exp(cum), s_enter)
    o = (o_intra + o_inter).reshape(b, l, h, dv)
    return o.astype(q.dtype), s_fin

def ssd_mixer(z, xbc, dt_raw, conv_buf, s0, p):
    b, l = z.shape[:2]
    xbc, conv_new = causal_conv(xbc, conv_buf, p['ssd_conv_w'], p['ssd_conv_b'])
    xbc = jax.nn.silu(xbc)
    xs, bm, cm = jnp.split(xbc, [SSD_WIDTH, SSD_WIDTH + SSD_GROUPS * SSD_STATE], axis=-1)
    rep = SSD_HEADS // SSD_GROUPS
    xs = xs.reshape(b, l, SSD_HEADS, HEAD_DIM)
    bm = jnp.repeat(bm.reshape(b, l, SSD_GROUPS, SSD_STATE), rep, axis=2)
    cm = jnp.repeat(cm.reshape(b, l, SSD_GROUPS, SSD_STATE), rep, axis=2)
    dt = jax.nn.softplus(dt_raw.astype(jnp.float32) + p['ssd_dt_bias'].astype(jnp.float32))
    log_a = -dt * jnp.exp(p['ssd_a_log'].astype(jnp.float32))
    y, s_new = chunk_scalar_decay(cm, bm, xs * dt[..., None].astype(xs.dtype), log_a, s0, SSD_CHUNK)
    y = (y + xs * p['ssd_d'][:, None]).reshape(b, l, SSD_WIDTH)
    y = rms_norm(y * jax.nn.silu(z), p['ssd_norm'])
    return y, conv_new, s_new

def retention_mixer(q, k, v, g, pos, s0, p):
    b, l = q.shape[:2]
    q = rotary(q.reshape(b, l, RET_HEADS, HEAD_DIM), pos)
    k = rotary(k.reshape(b, l, RET_HEADS, HEAD_DIM), pos) * (HEAD_DIM ** -0.5)
    v = v.reshape(b, l, RET_HEADS, HEAD_DIM)
    log_gamma = jnp.log(1.0 - 2.0 ** (-5.0 - jnp.arange(RET_HEADS, dtype=jnp.float32)))
    log_a = jnp.broadcast_to(log_gamma, (b, l, RET_HEADS))
    o, s_new = chunk_scalar_decay(q, k, v, log_a, s0, RET_CHUNK)
    of = o.astype(jnp.float32)
    mu = jnp.mean(of, axis=-1, keepdims=True)
    var = jnp.mean(jnp.square(of - mu), axis=-1, keepdims=True)
    on = ((of - mu) * lax.rsqrt(var + EPS)).reshape(b, l, RET_WIDTH) * p['ret_norm'].astype(jnp.float32)
    y = on.astype(g.dtype) * jax.nn.silu(g)
    return y, s_new

def gla_mixer(q, k, v, lr, r, s0, p):
    b, l = q.shape[:2]
    log_g = jax.nn.log_sigmoid((lr @ p['gla_w_gate2'] + p['gla_b_gate']).astype(jnp.float32)) / GLA_GATE_TEMP
    q = q.reshape(b, l, GLA_HEADS, GLA_DK) * (GLA_DK ** -0.5)
    k = k.reshape(b, l, GLA_HEADS, GLA_DK)
    v = v.reshape(b, l, GLA_HEADS, GLA_DV)
    o, s_new = chunk_vector_decay(q, k, v, log_g.reshape(b, l, GLA_HEADS, GLA_DK), s0, GLA_CHUNK)
    of = o.astype(jnp.float32)
    on = of * lax.rsqrt(jnp.mean(of * of, axis=-1, keepdims=True) + EPS)
    on = on.reshape(b, l, GLA_WIDTH) * p['gla_norm'].astype(jnp.float32)
    y = on.astype(r.dtype) * jax.nn.silu(r)
    return y, s_new

def rglru_mixer(yb, xb, conv_buf, h0, p):
    b, l = xb.shape[:2]
    gate = jax.nn.gelu(yb)
    xc, conv_new = causal_conv(xb, conv_buf, p['lru_conv_w'], p['lru_conv_b'])
    xh = xc.reshape(b, l, LRU_BLOCKS, LRU_BLOCK_DIM)
    r = jax.nn.sigmoid(jnp.einsum('blhi,hij->blhj', xh, p['lru_w_a']).reshape(b, l, LRU_WIDTH) + p['lru_b_a'])
    i = jax.nn.sigmoid(jnp.einsum('blhi,hij->blhj', xh, p['lru_w_x']).reshape(b, l, LRU_WIDTH) + p['lru_b_x'])
    log_a = -LRU_C * r.astype(jnp.float32) * jax.nn.softplus(-p['lru_lambda'].astype(jnp.float32))
    a = jnp.exp(log_a)
    u = jnp.sqrt(-jnp.expm1(2.0 * log_a)) * (i * xc).astype(jnp.float32)
    u = u.at[:, 0].add(a[:, 0] * h0.astype(jnp.float32))

    def combine(e1, e2):
        a1, b1 = e1
        a2, b2 = e2
        return a1 * a2, a2 * b1 + b2

    _, h = lax.associative_scan(combine, (a, u), axis=1)
    y = h.astype(xb.dtype) * gate
    return y, conv_new, h[:, -1]

def hybrid_layer(h, pos, states, p):
    ssd_conv, ssd_s, ret_s, gla_s, lru_conv, lru_h = states
    u = rms_norm(h, p['norm_mix']) @ p['w_in']
    (ssd_z, ssd_xbc, ssd_dt, ret_q, ret_k, ret_v, ret_g,
     gla_q, gla_k, gla_v, gla_lr, gla_r, lru_y, lru_x) = jnp.split(u, _split_points(), axis=-1)
    y_ssd, ssd_conv_new, ssd_s_new = ssd_mixer(ssd_z, ssd_xbc, ssd_dt, ssd_conv, ssd_s, p)
    y_ret, ret_s_new = retention_mixer(ret_q, ret_k, ret_v, ret_g, pos, ret_s, p)
    y_gla, gla_s_new = gla_mixer(gla_q, gla_k, gla_v, gla_lr, gla_r, gla_s, p)
    y_lru, lru_conv_new, lru_h_new = rglru_mixer(lru_y, lru_x, lru_conv, lru_h, p)
    mixed = jnp.concatenate([y_ssd, y_ret, y_gla, y_lru], axis=-1) @ p['w_out']
    h = h + mixed.astype(h.dtype)
    hn = rms_norm(h, p['norm_ffn'])
    h = h + ((jax.nn.silu(hn @ p['w_gate']) * (hn @ p['w_up'])) @ p['w_down']).astype(h.dtype)
    return h, (ssd_conv_new, ssd_s_new, ret_s_new, gla_s_new, lru_conv_new, lru_h_new)

def zero_states(b, dtype):
    f32 = jnp.float32
    return (jnp.zeros((b, CONV_WIDTH - 1, SSD_CONV_DIM), dtype),
            jnp.zeros((b, SSD_HEADS, SSD_STATE, HEAD_DIM), f32),
            jnp.zeros((b, RET_HEADS, HEAD_DIM, HEAD_DIM), f32),
            jnp.zeros((b, GLA_HEADS, GLA_DK, GLA_DV), f32),
            jnp.zeros((b, CONV_WIDTH - 1, LRU_WIDTH), dtype),
            jnp.zeros((b, LRU_WIDTH), f32))

def setup_inputs(seed: int = 0) -> dict:
    key = jax.random.key(seed)
    ks = iter(jax.random.split(key, 48))
    f32 = jnp.float32

    def nrm(shape, scale):
        return jax.random.normal(next(ks), shape, f32) * scale

    def gain(shape):
        return 1.0 + nrm(shape, 0.02)

    dt0 = jnp.exp(jax.random.uniform(next(ks), (DEPTH, SSD_HEADS), f32, math.log(1e-3), math.log(1e-1)))
    a0 = jax.random.uniform(next(ks), (DEPTH, LRU_WIDTH), f32, 0.9, 0.999) ** (1.0 / LRU_C)
    return {
        'x_prompt': nrm((BATCH, SEQ, D_MODEL), 1.0),
        'x_sample': nrm((DEC_BATCH, DEC_SEQ, D_MODEL), 1.0),
        'state_ssd_conv': nrm((DEPTH, DEC_BATCH, CONV_WIDTH - 1, SSD_CONV_DIM), 1.0),
        'state_ssd': nrm((DEPTH, DEC_BATCH, SSD_HEADS, SSD_STATE, HEAD_DIM), 0.1),
        'state_ret': nrm((DEPTH, DEC_BATCH, RET_HEADS, HEAD_DIM, HEAD_DIM), 0.5),
        'state_gla': nrm((DEPTH, DEC_BATCH, GLA_HEADS, GLA_DK, GLA_DV), 0.5),
        'state_lru_conv': nrm((DEPTH, DEC_BATCH, CONV_WIDTH - 1, LRU_WIDTH), 1.0),
        'state_lru': nrm((DEPTH, DEC_BATCH, LRU_WIDTH), 0.5),
        'norm_mix': gain((DEPTH, D_MODEL)),
        'w_in': nrm((DEPTH, D_MODEL, IN_DIM), D_MODEL ** -0.5),
        'ssd_conv_w': nrm((DEPTH, CONV_WIDTH, SSD_CONV_DIM), CONV_WIDTH ** -0.5),
        'ssd_conv_b': nrm((DEPTH, SSD_CONV_DIM), 0.02),
        'ssd_dt_bias': dt0 + jnp.log(-jnp.expm1(-dt0)),
        'ssd_a_log': jnp.log(jax.random.uniform(next(ks), (DEPTH, SSD_HEADS), f32, 1.0, 16.0)),
        'ssd_d': 1.0 + nrm((DEPTH, SSD_HEADS), 0.1),
        'ssd_norm': gain((DEPTH, SSD_WIDTH)),
        'ret_norm': gain((DEPTH, RET_WIDTH)),
        'gla_w_gate2': nrm((DEPTH, GLA_GATE_RANK, GLA_KEY_WIDTH), GLA_GATE_RANK ** -0.5),
        'gla_b_gate': nrm((DEPTH, GLA_KEY_WIDTH), 0.02),
        'gla_norm': gain((DEPTH, GLA_WIDTH)),
        'lru_conv_w': nrm((DEPTH, CONV_WIDTH, LRU_WIDTH), CONV_WIDTH ** -0.5),
        'lru_conv_b': nrm((DEPTH, LRU_WIDTH), 0.02),
        'lru_w_a': nrm((DEPTH, LRU_BLOCKS, LRU_BLOCK_DIM, LRU_BLOCK_DIM), LRU_BLOCK_DIM ** -0.5),
        'lru_b_a': nrm((DEPTH, LRU_WIDTH), 0.02),
        'lru_w_x': nrm((DEPTH, LRU_BLOCKS, LRU_BLOCK_DIM, LRU_BLOCK_DIM), LRU_BLOCK_DIM ** -0.5),
        'lru_b_x': nrm((DEPTH, LRU_WIDTH), 0.02),
        'lru_lambda': jnp.log(a0) - jnp.log1p(-a0),
        'w_out': nrm((DEPTH, D_MIX, D_MODEL), D_MIX ** -0.5),
        'norm_ffn': gain((DEPTH, D_MODEL)),
        'w_gate': nrm((DEPTH, D_MODEL, D_FF), D_MODEL ** -0.5),
        'w_up': nrm((DEPTH, D_MODEL, D_FF), D_MODEL ** -0.5),
        'w_down': nrm((DEPTH, D_FF, D_MODEL), D_FF ** -0.5),
        'norm_final': gain((D_MODEL,)),
    }

def reference(x_prompt, x_sample, state_ssd_conv, state_ssd, state_ret, state_gla, state_lru_conv, state_lru,
              norm_mix, w_in, ssd_conv_w, ssd_conv_b, ssd_dt_bias, ssd_a_log, ssd_d, ssd_norm, ret_norm,
              gla_w_gate2, gla_b_gate, gla_norm, lru_conv_w, lru_conv_b, lru_w_a, lru_b_a, lru_w_x, lru_b_x,
              lru_lambda, w_out, norm_ffn, w_gate, w_up, w_down, norm_final):
    bp, lp = x_prompt.shape[:2]
    ls = x_sample.shape[1]
    pos_prompt = jnp.arange(lp, dtype=jnp.int32)
    pos_sample = PAST_LEN + jnp.arange(ls, dtype=jnp.int32)
    prompt_init = zero_states(bp, x_prompt.dtype)
    hp, hs = x_prompt, x_sample
    new_p = [[] for _ in range(6)]
    new_s = [[] for _ in range(6)]
    for i in range(DEPTH):
        p = dict(norm_mix=norm_mix[i], w_in=w_in[i], ssd_conv_w=ssd_conv_w[i], ssd_conv_b=ssd_conv_b[i],
                 ssd_dt_bias=ssd_dt_bias[i], ssd_a_log=ssd_a_log[i], ssd_d=ssd_d[i], ssd_norm=ssd_norm[i],
                 ret_norm=ret_norm[i], gla_w_gate2=gla_w_gate2[i], gla_b_gate=gla_b_gate[i], gla_norm=gla_norm[i],
                 lru_conv_w=lru_conv_w[i], lru_conv_b=lru_conv_b[i], lru_w_a=lru_w_a[i], lru_b_a=lru_b_a[i],
                 lru_w_x=lru_w_x[i], lru_b_x=lru_b_x[i], lru_lambda=lru_lambda[i], w_out=w_out[i],
                 norm_ffn=norm_ffn[i], w_gate=w_gate[i], w_up=w_up[i], w_down=w_down[i])
        hp, st_p = hybrid_layer(hp, pos_prompt, prompt_init, p)
        sample_init = (state_ssd_conv[i], state_ssd[i], state_ret[i], state_gla[i], state_lru_conv[i], state_lru[i])
        hs, st_s = hybrid_layer(hs, pos_sample, sample_init, p)
        for j in range(6):
            new_p[j].append(st_p[j])
            new_s[j].append(st_s[j])
    y_prompt = rms_norm(hp, norm_final)
    y_sample = rms_norm(hs, norm_final)
    p_ssd_conv, p_ssd, p_ret, p_gla, p_lru_conv, p_lru = [jnp.stack(a, axis=0) for a in new_p]
    s_ssd_conv, s_ssd, s_ret, s_gla, s_lru_conv, s_lru = [jnp.stack(a, axis=0) for a in new_s]
    return (y_prompt, y_sample, p_ssd_conv, p_ssd, p_ret, p_gla, p_lru_conv, p_lru,
            s_ssd_conv, s_ssd, s_ret, s_gla, s_lru_conv, s_lru)


_drawn_inputs = setup_inputs


def setup_inputs(seed=0):
    import zlib

    import numpy as np

    out = dict(_drawn_inputs(seed))
    spreads = {}
    factors = {'ssd_d': 2.857,
     'ssd_norm': 4.116,
     'ret_norm': 7.301,
     'gla_b_gate': 6.334,
     'gla_norm': 7.547,
     'lru_b_a': 8.0,
     'lru_b_x': 8.0,
     'norm_ffn': 2.853,
     'norm_final': 2.739}
    for name, (base, spread) in spreads.items():
        noise = np.random.default_rng([zlib.crc32(name.encode()), seed]).standard_normal(out[name].shape)
        drawn = base * np.exp(spread * noise) if base else spread * noise
        out[name] = __import__('jax').numpy.asarray(drawn.astype(out[name].dtype))
    for name, factor in factors.items():
        out[name] = (out[name] * factor).astype(out[name].dtype)
    return out
```

```python
from contextlib import ExitStack

import numpy as np

import concourse.bass as bass
from concourse import mybir

ALU = mybir.AluOpType
ACT = mybir.ActivationFunctionType
AX_X = mybir.AxisListType.X
F32 = mybir.dt.float32
F32R = mybir.dt.float32r

P = 128
DM = 1024
KT = DM // P
DEPTH = 2
SEQ = 512
NSEQ = 8
SLEN = 4
NS = NSEQ * SLEN
TOK = SEQ + NS
HALF = TOK // 2
PAST = 4096
EPS = 1e-6
DFF = 2816
FT = DFF // P
CH = [(c, c * P, P) for c in range(SEQ // P)] + [(4, SEQ, NS)]
SAMPLE = 4
GDK = 32
CLAMP = 40.0 * 16.0

STREAM = 3 + SEQ + NSEQ * (3 + SLEN)
CW = STREAM - 3

IN_UNITS = [("misc", None), ("xbc", 256), ("xbc", 384), ("xbc", 512), ("xbc", 640), ("lx", 2836), ("lx", 2964),
            ("gq", 1796), ("gk", 1924), ("gv", 2052), ("gv", 2180), ("rk", 1028), ("rk", 1156),
            ("rq", 772), ("rq", 900), ("rv", 1284), ("rv", 1412), ("z", 0), ("z", 128),
            ("rg", 1540), ("rg", 1668), ("gr", 2324), ("gr", 2452), ("ly", 2580), ("ly", 2708)]
NIN = len(IN_UNITS)
OUT0 = NIN
FFN0 = OUT0 + KT
GROUP = KT
GU = 2 * GROUP + KT
NGRP = FT // GROUP
REST = FT - NGRP * GROUP
REST0 = FFN0 + NGRP * GU
NUNIT = REST0 + 2 * REST + KT
RING = 3
LU = -(-NUNIT // 6) * 6
PAD = LU - NUNIT
assert GU % RING == 0 and (FFN0 % RING, REST0 % RING) == (0, 0)

OUT_K = [0, 1, 4, 5, 6, 7, 2, 3]
G_SSD, G_RET, G_GLA, G_LRU = 0, 1, 2, 3


def columns(widths):
    at, out = 0, {}
    for name, w in widths:
        out[name] = (at, w)
        at += w
    return out, at


CONST, NCONST = columns([
    ("ident", P), ("upper", P), ("neg", P), ("keep", P), ("swap", P), ("centre", P), ("ones", P),
    ("ssd_blocks", 256), ("gla_blocks", 256), ("ret_blocks", P), ("ret_decay", 512), ("ret_q", 256),
    ("cos", TOK), ("sin", TOK), ("upper_s", NS + NSEQ), ("neg_s", NS), ("keep_s", NS), ("block_s", NS),
    ("seq_s", NSEQ), ("reset_s", NS), ("ret_decay_s", 4 * NS), ("ret_q_s", 2 * NS), ("ret_k", 4), ("ret_k_s", 4),
    ("ret_last", 2), ("ret_last_s", 2), ("gla_heads", 4), ("pair", 2)])

PARAM, NPARAM = columns([
    ("norm_ffn", 8), ("norm_next", 8), ("ssd_conv_w", 16), ("ssd_conv_b", 4), ("lru_conv_w", 8),
    ("lru_conv_b", 2), ("ssd_d", 2), ("ssd_norm", 2), ("ret_norm", 2), ("gla_norm", 2), ("gla_b", 1),
    ("lru_b_a", 2), ("lru_b_x", 2), ("lru_lambda", 2), ("dt_bias", 4), ("a_log", 4), ("lru_h0", 16),
    ("history", 6 * NSEQ * 3), ("lru_w", 512), ("gate2", P)])

SLOTS = {}


def at_slot(s, name, *args):
    SLOTS.setdefault(s, []).append((name, *args))


at_slot(2, "dt")
for _c in range(5):
    at_slot(12 + 2 * _c, "ssd_a", _c)
    at_slot(13 + 2 * _c, "ssd_b", _c)
    at_slot(27 + 2 * _c, "gla_a", _c)
    at_slot(28 + 2 * _c, "gla_b", _c)
    at_slot(39 + 2 * _c, "ret_a", _c)
    at_slot(40 + 2 * _c, "ret_b", _c)
at_slot(22, "lru_gates", 0)
at_slot(23, "lru_gates", 1)
at_slot(24, "gla_gate")
for _i, _s in enumerate((25, 26, 37, 38)):
    at_slot(_s, "rotate", _i)
for _i in range(2):
    at_slot(37 + 2 * _i, "z_gate", _i)
at_slot(38, "gla_stat")
for _i in range(3):
    at_slot(39 + _i, "gla_norm", _i)
at_slot(42, "ssd_stat")
for _i in range(2):
    at_slot(43 + _i, "ssd_norm", _i)
for _i in range(2):
    at_slot(45 + _i, "gla_out", _i)
    at_slot(47 + 2 * _i, "lru_out", _i)
for _n in ("centre", "ret_stat", "ret_norm"):
    at_slot(49, _n)
SLOTS[49].sort(key=lambda x: ["lru_out", "centre", "ret_stat", "ret_norm"].index(x[0]))


class Signal:

    def __init__(self, sem, per_layer, start=0):
        self.sem, self.per_layer, self.start = sem, per_layer, start

    def at(self, layer, n):
        return layer * self.per_layer + (self.start + n)


def trunk(nc, weights, params, consts, x, s_ssd, s_ret, s_gla, y, o_conv, o_ssd, o_ret, o_gla, o_lru,
          n_ssd, n_ret, n_gla):
    with ExitStack() as ctx:
        def sb(name, cols, dt=F32, parts=P):
            return ctx.enter_context(nc.sbuf_tensor(name, [parts, *cols], dt))

        def sem(name):
            return ctx.enter_context(nc.semaphore(name))

        def signal(name, per_layer, start=0):
            return Signal(sem(name), per_layer, start)

        h = sb("h", [KT, TOK])
        xh, xl = sb("xh", [KT, TOK], F32R), sb("xl", [KT, TOK], F32R)
        raw = sb("raw", [RING, KT * P])
        wh, wl = sb("wh", [RING, KT * P], F32R), sb("wl", [RING, KT * P], F32R)
        cs = sb("cs", [NCONST])
        pr = sb("pr", [NPARAM])
        rs_bcast = sb("rs_bcast", [TOK])
        misc = sb("misc", [TOK], parts=64)
        sp_x, sp_a, sp_e, sp_z = (sb(n, [22]) for n in ("sp_x", "sp_a", "sp_e", "sp_z"))
        sp_2, sp_p, sp_m, sp_y = (sb(n, [22]) for n in ("sp_2", "sp_p", "sp_m", "sp_y"))
        ssd_rate, log_a = sb("ssd_rate", [4]), sb("log_a", [5, 4])
        lru_neg, lru_pos = sb("lru_neg", [2]), sb("lru_pos", [2])
        cum_j, to_last = sb("cum_j", [8]), sb("to_last", [2, 4])
        gla_last = sb("gla_last", [2, NSEQ])
        rstd = sb("rstd", [20])
        PT = sb("PT", [4, P])
        D = sb("D", [4, P])
        kz = sb("kz", [4, P])
        qt = sb("qt", [2, 2, P])
        E = sb("E", [2, P])
        ge = sb("ge", [3, P])
        V, K, Vd = sb("V", [256]), sb("K", [256]), sb("Vd", [256])
        dS = sb("dS", [256])
        S_ssd, S_gla, S_ret = sb("S_ssd", [256]), sb("S_gla", [256]), sb("S_ret", [256])
        S0 = sb("S0", [1024])
        Vx = sb("Vx", [1024 + 2 * TOK])
        S1 = Vx[:, 0:1024]
        sq = Vx[:, 1024:1024 + 2 * TOK].rearrange("p (t n) -> p t n", t=2)
        gqkc = sb("gqkc", [3, TOK])
        ret_gate = gqkc[:, 0:2, :]
        gv = sb("gv", [2, TOK])
        rq, rk, rv = sb("rq", [2, TOK]), sb("rk", [2, TOK]), sb("rv", [2, TOK])
        hl = sb("hl", [2, STREAM])
        tz = sb("tz", [2, TOK])
        conv_out = sb("conv_out", [6, 27])
        lru_last = sb("lru_last", [2, 1 + NSEQ])

        early = ExitStack()
        xbc = early.enter_context(nc.sbuf_tensor("xbc", [P, 4, TOK], F32))
        early.close()
        gh, gl = [None] * 4, [None] * 4
        gh[G_RET], gl[G_RET] = sb("gh_ret", [2, TOK], F32R), sb("gl_ret", [2, TOK], F32R)
        early = ExitStack()
        cbuf = early.enter_context(nc.sbuf_tensor("cbuf", [P, 3, STREAM], F32))
        ct = early.enter_context(nc.sbuf_tensor("ct", [P, 2, STREAM], F32))
        lru_g, lru_a, lru_m, lru_u = (early.enter_context(nc.sbuf_tensor(n, [P, STREAM], F32))
                                      for n in ("lru_g", "lru_a", "lru_m", "lru_u"))
        lru_x = early.enter_context(nc.sbuf_tensor("lru_x", [P, 2, STREAM], F32))
        early.close()
        for n, i in (("ssd", G_SSD), ("gla", G_GLA), ("lru", G_LRU)):
            gh[i], gl[i] = sb("gh_" + n, [2, TOK], F32R), sb("gl_" + n, [2, TOK], F32R)

        bank = [ctx.enter_context(nc.psum_tensor(f"bank{i}", [P, 512], F32)) for i in range(8)]
        dense, M = bank[0:3], bank[3:8]

        def cst(name, parts=P, lo=0, n=None):
            at, w = CONST[name]
            return cs[0:parts, at + lo:at + (w if n is None else lo + n)]

        def par(name, i=0, n=1):
            at, _ = PARAM[name]
            return pr[:, at + i:at + i + n]

        def masks(c, name):
            return cst(name + "_s" if c == SAMPLE else name, CH[c][2])

        in_loaded = sem("in_loaded")
        raw_loaded = [sem(f"raw_loaded{i}") for i in range(RING)]
        hi_done, lo_done = sem("hi_done"), sem("lo_done")
        dense_done = sem("dense_done")
        dense_free = Signal(sem("dense_free"), 2 * LU, 3)
        params_free = signal("params_free", 1, 1)
        params_loaded = signal("params_loaded", 16)
        s0_loaded = signal("s0_loaded", 48)
        stored = sem("stored")
        STORES = 8 * 16
        h_new = signal("h_new", 2 * KT)
        h_squared = signal("h_squared", 2 * KT, KT)
        xl_done = signal("xl_done", 2 * KT, KT)
        stat_done = signal("stat_done", 2 * KT, KT)
        mean_done = signal("mean_done", 2, 1)
        root_done = signal("root_done", 2, 1)
        rstd_done = signal("rstd_done", 2, 1)
        rs_spread = signal("rs_spread", 2, 1)
        gate_out = signal("gate_out", FT)
        gate_silu = signal("gate_silu", FT)
        act_out = signal("act_out", FT)
        act_hi = signal("act_hi", FT)
        act_lo = signal("act_lo", FT)
        dt_out, dt_turned, sp_in, sp_exp = (signal(n, 1) for n in ("dt_out", "dt_turned", "sp_in", "sp_exp"))
        dt_ready = signal("dt_ready", 1)
        conv_done = signal("conv_done", 6)
        conv_silu = signal("conv_silu", 4)
        ssd_a, ssd_cj, ssd_dm, ssd_e, ssd_dx, ssd_bin, ssd_b, ssd_s = (
            signal(n, 5) for n in ("ssd_a", "ssd_cj", "ssd_dm", "ssd_e", "ssd_dx", "ssd_bin", "ssd_b", "ssd_s"))
        lru_mm, lru_sig, lru_prod, lru_root, lru_free = (
            signal(n, 2) for n in ("lru_mm", "lru_sig", "lru_prod", "lru_root", "lru_free"))
        gla_gmm, gla_ge, gla_cum, gla_qkv = (signal(n, 1) for n in ("gla_gmm", "gla_ge", "gla_cum", "gla_qkv"))
        gla_diff, gla_exp, gla_pre, gla_a, gla_bin, gla_b, gla_s, gla_o = (
            signal(n, 5) for n in ("gla_diff", "gla_exp", "gla_pre", "gla_a", "gla_bin", "gla_b", "gla_s", "gla_o"))
        rot_in, rot_mm, rot_out = (signal(n, 4) for n in ("rot_in", "rot_mm", "rot_out"))
        ret_v = signal("ret_v", 1)
        ret_a, ret_bin, ret_b, ret_s = (signal(n, 5) for n in ("ret_a", "ret_bin", "ret_b", "ret_s"))
        gate_in = signal("gate_in", 8)
        gate_act = signal("gate_act", 8)
        y_out = signal("y_out", 8)
        y_hi = signal("y_hi", 8)
        y_lo = signal("y_lo", 8)
        n_in = signal("n_in", 1)
        n_sq, n_mm, n_mean, n_root, n_rstd = (
            signal(n, 3) for n in ("n_sq", "n_mm", "n_mean", "n_root", "n_rstd"))
        n_spread = signal("n_spread", 6)
        n_used = signal("n_used", 6)
        cent_mm, cent_out = signal("cent_mm", 1), signal("cent_out", 1)
        y_final, y_stored = sem("y_final"), sem("y_stored")

        def operand(k):
            return gh[k // 2][:, k % 2, :], gl[k // 2][:, k % 2, :]

        def samples(row, first, n=SLEN):
            return row[:, 3 + SEQ:STREAM].rearrange("p (b l) -> p b l", b=NSEQ)[:, :, first:first + n]

        def by_sequence(cols):
            return cols.rearrange("p (b l) -> p b l", b=NSEQ)

        block = ctx.enter_context(nc.Block())

        @block.sync
        def _(sp):
            sp.dma_start(h[:], x).then_inc(in_loaded, 16)
            sp.dma_start(cs[:], consts[:, 0:NCONST]).then_inc(in_loaded, 16)
            sp.dma_start(tz[:, 0, 0:KT], consts[:, NCONST:NCONST + KT]).then_inc(in_loaded, 16)
            for s in range(RING):
                sp.dma_start(raw[:, s, :], weights[s]).then_inc(raw_loaded[s], 16)
            with sp.Fori(0, DEPTH * LU // RING) as turn:
                for s in range(RING):
                    sp.wait_ge(lo_done, turn * RING + (s + 1))
                    sp.dma_start(raw[:, s, :], weights[turn * RING + (s + RING)]).then_inc(raw_loaded[s], 16)
            for s in range(RING):
                sp.wait_ge(raw_loaded[s], 16 * (DEPTH * LU // RING + 1))
            sp.wait_ge(y_final, KT)
            sp.dma_start(y, h[:]).then_inc(y_stored, 16)
            sp.wait_ge(y_stored, 16)
            sp.wait_ge(stored, DEPTH * STORES)

        @block.gpsimd
        def _(pool):
            def split(s, n):
                pool.wait_ge(hi_done, n + 1)
                nc.gpsimd.tensor_tensor(wl[:, s, :], raw[:, s, :], wh[:, s, :].bitcast(F32),
                                        ALU.subtract).then_inc(lo_done, 1)

            for s in range(RING):
                split(s, s)
            with pool.Fori(0, DEPTH * LU // RING) as turn:
                for s in range(RING):
                    split(s, turn * RING + (s + RING))

        @block.scalar
        def _(act):
            a = nc.scalar.activation

            def hi_first(s):
                act.wait_ge(raw_loaded[s], 16)
                a(wh[:, s, :], raw[:, s, :], ACT.Copy).then_inc(hi_done, 1)

            def hi_ahead(layer, u):
                s = u % RING
                act.wait_ge(raw_loaded[s], layer * (16 * LU // RING) + 16 * (u // RING + 2))
                act.wait_ge(dense_done, layer * (2 * LU) + 2 * (u + 1))
                a(wh[:, s, :], raw[:, s, :], ACT.Copy).then_inc(hi_done, 1)

            def hi_ahead_group(layer, g, i):
                s = i % RING
                act.wait_ge(raw_loaded[s], layer * (16 * LU // RING) + g * (16 * GU // RING)
                            + 16 * ((FFN0 + i) // RING + 2))
                act.wait_ge(dense_done, layer * (2 * LU) + g * (2 * GU) + 2 * (FFN0 + i + 1))
                a(wh[:, s, :], raw[:, s, :], ACT.Copy).then_inc(hi_done, 1)

            def next_operand(layer, i, m, gain):
                act.wait_ge(h_new.sem, h_new.at(layer, i * KT + m + 1))
                if m >= 2:
                    act.wait_ge(stat_done.sem, stat_done.at(layer, i * KT + m - 1))
                a(sq[:, m % 2, :], h[:, m, :], ACT.Square)
                a(xh[:, m, :], h[:, m, :], ACT.Copy, scale=gain(m)).then_inc(h_squared.sem, 1)

            def root(layer, i):
                act.wait_ge(mean_done.sem, mean_done.at(layer, i + 1))
                a(rstd[:, 0:5], rstd[:, 0:5], ACT.Sqrt).then_inc(root_done.sem, 1)

            for s in range(RING):
                hi_first(s)
            act.wait_ge(in_loaded, 48)
            for m in range(KT):
                if m >= 2:
                    act.wait_ge(stat_done.sem, m - 1)
                a(sq[:, m % 2, :], h[:, m, :], ACT.Square)
                a(xh[:, m, :], h[:, m, :], ACT.Copy, scale=tz[:, 0, m:m + 1]).then_inc(h_squared.sem, 1)
            act.wait_ge(mean_done.sem, 1)
            a(rstd[:, 0:5], rstd[:, 0:5], ACT.Sqrt).then_inc(root_done.sem, 1)

            with act.Fori(0, DEPTH) as layer:
                act.wait_ge(params_free.sem, params_free.at(layer, 0))
                act.dma_start(pr[:], params[layer]).then_inc(params_loaded.sem, 16)
                act.dma_start(S0[:], s_ssd[layer]).then_inc(s0_loaded.sem, 16)

                def dt(_=None):
                    act.wait_ge(params_loaded.sem, params_loaded.at(layer, 16))
                    a(ssd_rate[:], par("a_log", 0, 4), ACT.Exp)
                    act.wait_ge(sp_in.sem, sp_in.at(layer, 1))
                    a(sp_a[:], sp_x[:], ACT.Abs)
                    act.drain()
                    a(sp_e[:], sp_a[:], ACT.Exp, scale=-1.0).then_inc(sp_exp.sem, 1)

                def silu_conv(t):
                    act.wait_ge(conv_done.sem, conv_done.at(layer, t + 1))
                    a(xbc[:, t, 0:SEQ], ct[:, t % 2, 0:SEQ], ACT.Silu)
                    a(by_sequence(xbc[:, t, SEQ:TOK]), samples(ct[:, t % 2, :], 0), ACT.Silu).then_inc(conv_silu.sem, 1)

                def ssd_a_(c):
                    n = CH[c][2]
                    w = NS + NSEQ if c == SAMPLE else P
                    act.wait_ge(ssd_cj.sem, ssd_cj.at(layer, c + 1))
                    a(E[:, :, 0:w], M[1][:, 0:256].rearrange("p (r i) -> p r i", r=2)[:, :, 0:w],
                      ACT.Exp)
                    a(to_last[0:n, 1, :], to_last[0:n, 0, :], ACT.Exp).then_inc(ssd_e.sem, 1)
                    act.wait_ge(ssd_dm.sem, ssd_dm.at(layer, c + 1))
                    a(D[0:n, :, 0:n], D[0:n, :, 0:n], ACT.Exp).then_inc(ssd_dx.sem, 1)

                def lru_gates(t):
                    act.wait_ge(lru_mm.sem, lru_mm.at(layer, t + 1))
                    if t:
                        act.wait_ge(lru_free.sem, lru_free.at(layer, t))
                    for b in range(2):
                        a(lru_m[:, b * (CW // 2):(b + 1) * (CW // 2)], M[b][:, 0:CW // 2], ACT.Sigmoid,
                          bias=par("lru_b_a", t))
                    for b in range(2):
                        a(lru_g[:, b * (CW // 2):(b + 1) * (CW // 2)], M[2 + b][:, 0:CW // 2], ACT.Sigmoid,
                          bias=par("lru_b_x", t))
                    act.drain()
                    a(lru_a[:, 0:CW], lru_m[:, 0:CW], ACT.Exp, scale=lru_neg[:, t:t + 1])
                    a(lru_u[:, 0:CW], lru_m[:, 0:CW], ACT.Tanh, scale=lru_pos[:, t:t + 1]).then_inc(lru_sig.sem, 1)
                    act.wait_ge(lru_prod.sem, lru_prod.at(layer, t + 1))
                    a(lru_m[:, 0:CW], lru_m[:, 0:CW], ACT.Sqrt).then_inc(lru_root.sem, 1)

                def gla_gate(_=None):
                    act.wait_ge(gla_gmm.sem, gla_gmm.at(layer, 1))
                    for b in range(2):
                        a(tz[:, 0, b * HALF:(b + 1) * HALF], M[b][:, 0:HALF], ACT.Identity, bias=par("gla_b"))
                    act.drain()
                    a(tz[:, 1, :], tz[:, 0, :], ACT.Abs)
                    act.drain()
                    a(tz[:, 1, :], tz[:, 1, :], ACT.Exp, scale=-1.0)
                    act.drain()
                    a(tz[:, 1, :], tz[:, 1, :], ACT.Ln, bias=1.0).then_inc(gla_ge.sem, 1)

                def gla_pre_(c):
                    n = CH[c][2]
                    act.wait_ge(gla_diff.sem, gla_diff.at(layer, c + 1))
                    s = 1.0 / 16.0
                    if c < SAMPLE:
                        a(D[:], D[:], ACT.Exp, scale=s)
                        a(gla_last[:, c % 2, 0:1], gqkc[:, 2, CH[c][1] + P - 1:CH[c][1] + P], ACT.Exp, scale=s)
                    else:
                        a(gla_last[:, c % 2, :], gqkc[:, 2, SEQ + SLEN - 1:TOK:SLEN], ACT.Exp, scale=s)
                    a(ge[:, :, 0:n], ge[:, :, 0:n], ACT.Exp, scale=s).then_inc(gla_exp.sem, 1)

                def gla_b_(c):
                    _, off, n = CH[c]
                    act.wait_ge(gla_b.sem, gla_b.at(layer, c + 1))
                    for t in range(2):
                        src = M[2][:, t * P:t * P + n] if c < SAMPLE else M[2 + t][:, 0:n]
                        ins = a(gv[:, t, off:off + n], src, ACT.Copy)
                    ins.then_inc(gla_o.sem, 1)

                def gate(i, func):
                    act.wait_ge(gate_in.sem, gate_in.at(layer, i + 1))
                    buf = ret_gate if i in (2, 3) else tz
                    a(buf[:, i % 2, :], buf[:, i % 2, :], func).then_inc(gate_act.sem, 1)

                def norm_root(i, n):
                    act.wait_ge(n_mean.sem, n_mean.at(layer, i + 1))
                    a(rstd[:, 0:n], rstd[:, 0:n], ACT.Sqrt).then_inc(n_root.sem, 1)

                def squares(src):
                    a(sq, src, ACT.Square).then_inc(n_sq.sem, 1)

                def high(i, g, t, src):
                    act.wait_ge(y_out.sem, y_out.at(layer, i + 1))
                    a(gh[g][:, t, :], src, ACT.Copy).then_inc(y_hi.sem, 1)

                def gla_stat(_=None):
                    act.drain()
                    act.wait_ge(rot_out.sem, rot_out.at(layer, 4))
                    squares(gv[:])
                    norm_root(0, 20)

                def ssd_stat(_=None):
                    act.wait_ge(n_in.sem, n_in.at(layer, 1))
                    squares(xbc[:, 0:2, :])
                    norm_root(1, 5)

                def ssd_norm(i):
                    if i == 1:
                        high(0, G_SSD, 0, xbc[:, 0, :])
                        high(1, G_SSD, 1, xbc[:, 1, :])

                def ret_stat(_=None):
                    act.wait_ge(cent_out.sem, cent_out.at(layer, 1))
                    squares(rv[:])
                    norm_root(2, 20)

                def ret_norm(_=None):
                    high(6, G_RET, 0, rv[:, 0, :])
                    high(7, G_RET, 1, rv[:, 1, :])

                stages = {
                    "dt": dt, "ssd_a": ssd_a_, "lru_gates": lru_gates, "gla_gate": gla_gate, "gla_b": gla_b_,
                    "z_gate": lambda t: None, "gla_stat": gla_stat, "ssd_stat": ssd_stat, "ssd_norm": ssd_norm,
                    "gla_out": lambda t: high(2 + t, G_GLA, t, tz[:, t, :]),
                    "lru_out": lambda t: high(4 + t, G_LRU, t, tz[:, t, :]),
                    "ret_stat": ret_stat, "ret_norm": ret_norm,
                }

                for s in range(2 * NIN):
                    u = s // 2
                    if s % 2:
                        hi_ahead(layer, u)
                        name = IN_UNITS[u][0]
                        if name == "xbc":
                            silu_conv(u - 1)
                        if name in ("z", "rg", "gr", "ly"):
                            gate(u - 17, ACT.Gelu_apprx_tanh if name == "ly" else ACT.Silu)
                    for name, *args in SLOTS.get(s, []):
                        if name in stages:
                            stages[name](*args)
                        if (name, *args) == ("ssd_b", SAMPLE):
                            act.wait_ge(ssd_s.sem, ssd_s.at(layer, 5))
                            act.dma_start(o_ssd[layer], S_ssd[:]).then_inc(stored, 16)
                            act.dma_start(n_ssd[layer], S1).then_inc(stored, 16)
                            act.dma_start(o_conv[layer], conv_out[:]).then_inc(stored, 16)
                            act.dma_start(S0[:, 0:512], s_gla[layer]).then_inc(s0_loaded.sem, 16)
                        if name == "gla_gate":
                            act.wait_ge(lru_free.sem, lru_free.at(layer, 2))
                            act.dma_start(o_lru[layer], lru_last[:]).then_inc(stored, 16)
                            gla_pre_(0)
                        if name == "gla_a" and args[0] < SAMPLE:
                            gla_pre_(args[0] + 1)
                        if (name, *args) == ("gla_b", SAMPLE):
                            act.wait_ge(gla_s.sem, gla_s.at(layer, 5))
                            act.dma_start(o_gla[layer], S_gla[:]).then_inc(stored, 16)
                            act.dma_start(n_gla[layer], S1[:, 0:512]).then_inc(stored, 16)
                            act.dma_start(S0[:], s_ret[layer]).then_inc(s0_loaded.sem, 16)
                        if (name, *args) == ("ret_b", SAMPLE):
                            act.wait_ge(ret_s.sem, ret_s.at(layer, 5))
                            act.dma_start(o_ret[layer], S_ret[:]).then_inc(stored, 16)
                            act.dma_start(n_ret[layer], S1).then_inc(stored, 16)

                for m in range(KT):
                    hi_ahead(layer, OUT0 + m)
                    next_operand(layer, 0, m, lambda m: par("norm_ffn", m))
                root(layer, 0)

                def ffn_unit(i, count):
                    if i % 2 == 0:
                        act.wait_ge(gate_out.sem, count)
                        a(tz[:, 0, :], tz[:, 0, :], ACT.Silu).then_inc(gate_silu.sem, 1)
                    else:
                        act.wait_ge(act_out.sem, count)
                        a(operand(i // 2)[0], tz[:, 1, :], ACT.Copy).then_inc(act_hi.sem, 1)

                with act.Fori(0, NGRP) as g:
                    for i in range(GU):
                        hi_ahead_group(layer, g, i)
                        if i < 2 * GROUP:
                            ffn_unit(i, layer * FT + g * GROUP + (i // 2 + 1))
                for i in range(2 * REST + KT):
                    hi_ahead(layer, REST0 + i)
                    if i < 2 * REST:
                        ffn_unit(i, layer * FT + (NGRP * GROUP + i // 2 + 1))
                    if i >= 2 * REST:
                        next_operand(layer, 1, i - 2 * REST, lambda m: par("norm_next", m))
                for i in range(PAD):
                    hi_ahead(layer, NUNIT + i)
                root(layer, 1)
                act.wait_ge(stored, (layer + 1) * STORES)

        @block.vector
        def _(dve):
            v = nc.vector
            tt, ts, stt, copy = v.tensor_tensor, v.tensor_scalar, v.scalar_tensor_tensor, v.tensor_copy

            def bc(ap, *shape):
                return ap.to_broadcast([ap.shape[0], *shape])

            def rms_rstd(layer, i):
                dve.wait_ge(stat_done.sem, stat_done.at(layer, (i + 1) * KT))
                sums = M[4][:, 0:5 * KT].rearrange("p (m c) -> p c m", c=5)
                v.tensor_reduce(rstd[:, 0:4], sums[:, 0:4, :], AX_X, ALU.add)
                v.tensor_reduce(rstd[0:NS, 4:5], sums[0:NS, 4:5, :], AX_X, ALU.add)
                dve.drain()
                ts(rstd[:, 0:4], rstd[:, 0:4], 1.0 / DM, EPS, ALU.mult, ALU.add)
                ts(rstd[0:NS, 4:5], rstd[0:NS, 4:5], 1.0 / DM, EPS, ALU.mult, ALU.add).then_inc(mean_done.sem, 1)
                dve.wait_ge(root_done.sem, root_done.at(layer, i + 1))
                v.reciprocal(rstd[:, 0:5], rstd[:, 0:5]).then_inc(rstd_done.sem, 1)
                dve.wait_ge(rs_spread.sem, rs_spread.at(layer, i + 1))
                copy(rs_bcast[:, 0:SEQ], M[0][:])
                copy(rs_bcast[:, SEQ:TOK], M[1][:, 0:NS])
                dve.drain()

            def xl_tile(layer, i, m, gain):
                dve.wait_ge(h_squared.sem, h_squared.at(layer, i * KT + m + 1))
                stt(xl[:, m, :], h[:, m, :], gain, xh[:, m, :].bitcast(F32), ALU.mult,
                    ALU.subtract).then_inc(xl_done.sem, 1)

            v.memset(sp_x[:], 0.0).then_inc(dense_free.sem, 3)
            v.memset(rstd[:], 1.0)
            dve.drain().then_inc(params_free.sem, 1)
            dve.wait_ge(in_loaded, 48)
            for m in range(KT):
                dve.wait_ge(h_squared.sem, m + 1)
                stt(xl[:, m, :], h[:, m, :], tz[:, 0, m:m + 1], xh[:, m, :].bitcast(F32), ALU.mult,
                    ALU.subtract).then_inc(xl_done.sem, 1)
            rms_rstd(0, -1)

            with dve.Fori(0, DEPTH) as layer:

                def take(u, half):
                    q = 2 * u + half
                    dve.wait_ge(dense_done, layer * (2 * LU) + (q + 1))
                    return dense[q % 3][:, 0:HALF], slice(half * HALF, (half + 1) * HALF)

                def conv(t, half):
                    u, slot = 1 + t, t % 3
                    acc, cols = take(u, half)
                    row = cbuf[:, slot, :]
                    if half == 0:
                        if t == 0:
                            dve.wait_ge(params_loaded.sem, params_loaded.at(layer, 16))
                        v.memset(row[:, 0:3], 0.0)
                        copy(samples(row, 0, 3), par("history", t * 24, 24).rearrange("p (b l) -> p b l", b=NSEQ))
                        tt(row[:, 3:3 + HALF], acc, rs_bcast[:, cols], ALU.mult).then_inc(dense_free.sem, 1)
                        return
                    n = SEQ - HALF
                    tt(row[:, 3 + HALF:3 + SEQ], acc[:, 0:n], rs_bcast[:, HALF:SEQ], ALU.mult)
                    tt(samples(row, 3), by_sequence(acc[:, n:HALF]), by_sequence(rs_bcast[:, SEQ:TOK]),
                       ALU.mult).then_inc(dense_free.sem, 1)
                    dve.drain()
                    copy(conv_out[:, t, 0:3], row[:, SEQ:SEQ + 3])
                    copy(conv_out[:, t, 3:27].rearrange("p (b l) -> p b l", b=NSEQ), samples(row, 4, 3))
                    w, b = ("ssd_conv_w", par("ssd_conv_b", t)) if t < 4 else ("lru_conv_w", par("lru_conv_b", t - 4))
                    out = (ct[:, t % 2, :] if t < 4 else lru_x[:, t - 4, :])[:, 0:CW]
                    if 2 <= t < 4:
                        dve.wait_ge(conv_silu.sem, conv_silu.at(layer, t - 1))
                    ts(out, row[:, 0:CW], par(w, 4 * (t % 4)), b, ALU.mult, ALU.add)
                    for j in range(1, 4):
                        dve.drain()
                        ins = stt(out, row[:, j:j + CW], par(w, 4 * (t % 4) + j), out, ALU.mult, ALU.add)
                    ins.then_inc(conv_done.sem, 1)

                def evacuate(u, half):
                    name = IN_UNITS[u][0]
                    if name in ("xbc", "lx"):
                        return conv(u - 1, half)
                    if half == 0 and name in ("z", "gr", "ly"):
                        dve.drain()
                    acc, cols = take(u, half)
                    if name == "misc":
                        ins = tt(misc[:, cols], acc[0:64], rs_bcast[0:64, cols], ALU.mult)
                        ins.then_inc(dense_free.sem, 1)
                        if half:
                            dve.drain().then_inc(dt_out.sem, 1)
                        return
                    if name == "gq":
                        stt(gqkc[:, 0, cols], acc, GDK ** -0.5, rs_bcast[:, cols], ALU.mult,
                            ALU.mult).then_inc(dense_free.sem, 1)
                        return
                    first = [n for n, _ in IN_UNITS].index(name)
                    dst = {"gk": gqkc[:, 1:2, :], "gv": gv, "rk": rk, "rq": rq, "rv": rv, "z": tz, "rg": ret_gate,
                           "gr": tz, "ly": tz}[name][:, u - first, cols]
                    tt(dst, acc, rs_bcast[:, cols], ALU.mult).then_inc(dense_free.sem, 1)
                    if half and name in ("rk", "rq"):
                        dve.drain().then_inc(rot_in.sem, 1)
                    if half and name in ("z", "rg", "gr", "ly"):
                        dve.drain().then_inc(gate_in.sem, 1)

                def by_seq_values(src):
                    tt(Vx[0:NS, 0:2048].rearrange("p (h b d) -> p h b d", h=4, b=NSEQ),
                       src[0:NS, :].rearrange("p (h d) -> p h d", h=4).unsqueeze(2).to_broadcast([NS, 4, NSEQ, 64]),
                       cst("seq_s", NS).unsqueeze(1).unsqueeze(3).to_broadcast([NS, 4, NSEQ, 64]), ALU.mult)

                def heads(ap):
                    return ap.rearrange("p (h d) -> p h d", h=4)

                def per_head(ap4, n, d):
                    return ap4.unsqueeze(2).to_broadcast([n, 4, d])

                def dt(_=None):
                    dve.wait_ge(dt_turned.sem, dt_turned.at(layer, 1))
                    bias = par("dt_bias", 0, 4)
                    tt(sp_x[:, 0:16].rearrange("p (c h) -> p c h", h=4), M[4][:, 0:16].rearrange("p (c h) -> p c h", h=4),
                       bias.unsqueeze(1).to_broadcast([P, 4, 4]), ALU.add)
                    tt(sp_x[0:NS, 16:20], M[4][0:NS, 16:20], bias[0:NS], ALU.add)
                    ts(sp_x[:, 20:22], par("lru_lambda", 0, 2), -1.0, None, ALU.mult)
                    dve.drain().then_inc(sp_in.sem, 1)
                    ts(sp_m[:], sp_x[:], 0.0, None, ALU.max)
                    dve.wait_ge(sp_exp.sem, sp_exp.at(layer, 1))
                    ts(sp_z[:], sp_e[:], 2.0, None, ALU.add)
                    dve.drain()
                    v.reciprocal(sp_z[:], sp_z[:])
                    dve.drain()
                    tt(sp_z[:], sp_z[:], sp_e[:], ALU.mult)
                    dve.drain()
                    tt(sp_2[:], sp_z[:], sp_z[:], ALU.mult)
                    dve.drain()
                    ts(sp_p[:], sp_2[:], 1.0 / 15.0, None, ALU.mult)
                    for k in (13, 11, 9, 7, 5, 3):
                        dve.drain()
                        stt(sp_p[:], sp_p[:], 1.0 / k, sp_2[:], ALU.add, ALU.mult)
                    dve.drain()
                    stt(sp_p[:], sp_p[:], 1.0, sp_z[:], ALU.add, ALU.mult)
                    dve.drain()
                    stt(sp_y[:], sp_p[:], 2.0, sp_m[:], ALU.mult, ALU.add)
                    dve.drain()
                    stt(log_a[:], sp_y[:, 0:20].rearrange("p (c h) -> p c h", h=4), -1.0,
                        ssd_rate[:].unsqueeze(1).to_broadcast([P, 5, 4]), ALU.mult, ALU.mult)
                    ts(lru_neg[:], sp_y[:, 20:22], -8.0, None, ALU.mult)
                    ts(lru_pos[:], sp_y[:, 20:22], 8.0, None, ALU.mult)
                    dve.drain().then_inc(dt_ready.sem, 1)

                def ssd_a_(c):
                    _, off, n = CH[c]
                    dve.wait_ge(ssd_a.sem, ssd_a.at(layer, c + 1))
                    copy(cum_j[0:n, :], M[1][0:n, 256:264])
                    dve.drain()
                    tt(to_last[0:n, 0, :], cum_j[0:n, 4:8], cum_j[0:n, 0:4], ALU.subtract)
                    dve.drain().then_inc(ssd_cj.sem, 1)
                    for hd in range(4):
                        ins = stt(D[0:n, hd, 0:n], M[0][0:n, hd * P:hd * P + n], cum_j[0:n, hd:hd + 1],
                                  masks(c, "neg"), ALU.subtract, ALU.min)
                    ins.then_inc(ssd_dm.sem, 1)
                    tt(heads(V[0:n, :]), heads(M[2][0:n, 128:384]), per_head(sp_y[0:n, 4 * c:4 * c + 4], n, 64), ALU.mult)
                    copy(K[0:n, 0:P], M[2][0:n, 384:512])
                    dve.wait_ge(ssd_e.sem, ssd_e.at(layer, c + 1))
                    tt(qt[:, c % 2, :, 0:n], E[:, :, 0:n], xbc[:, 3, off:off + n].unsqueeze(1).to_broadcast([P, 2, n]),
                       ALU.mult)
                    dve.drain()
                    tt(heads(Vd[0:n, :]), heads(V[0:n, :]), per_head(to_last[0:n, 1, :], n, 64), ALU.mult)
                    if c == SAMPLE:
                        dve.drain()
                        by_seq_values(Vd)
                    dve.wait_ge(ssd_dx.sem, ssd_dx.at(layer, c + 1))
                    for g in range(2):
                        tt(PT[0:n, 2 * g:2 * g + 2, 0:n], D[0:n, 2 * g:2 * g + 2, 0:n],
                           M[2 + g][0:n, 0:n].unsqueeze(1).to_broadcast([n, 2, n]), ALU.mult)
                    dve.drain().then_inc(ssd_bin.sem, 1)

                def ssd_b_(c):
                    _, off, n = CH[c]
                    dve.wait_ge(ssd_b.sem, ssd_b.at(layer, c + 1))
                    for g in range(2):
                        xs = xbc[:, g, off:off + n]
                        stt(xs, xs, par("ssd_d", g), M[g][:, 0:n], ALU.mult, ALU.add)
                    if c == SAMPLE:
                        dve.wait_ge(s0_loaded.sem, s0_loaded.at(layer, 16))
                        tt(S1.rearrange("p (r b d) -> p r b d", r=2, b=NSEQ),
                           S0[:].rearrange("p (r b d) -> p r b d", r=2, b=NSEQ),
                           E[:, :, NS:NS + NSEQ].unsqueeze(3).to_broadcast([P, 2, NSEQ, 64]), ALU.mult)
                        dve.drain()
                        for r in range(2):
                            tt(S1[:, 512 * r:512 * r + 512], S1[:, 512 * r:512 * r + 512], M[2 + r][:], ALU.add)
                    else:
                        tt((S_ssd if c == 0 else dS)[:], M[2][:, 0:256], cst("ssd_blocks"), ALU.mult)
                        if c:
                            dve.drain()
                            for r in range(2):
                                new, old = (x[:].rearrange("p (g r d) -> p g r d", g=2, r=2)[:, :, r, :] for x in (dS, S_ssd))
                                stt(old, old, E[:, r, P - 1:P], new, ALU.mult, ALU.add)
                    dve.drain().then_inc(ssd_s.sem, 1)

                def lru_gates(t):
                    dve.wait_ge(lru_sig.sem, lru_sig.at(layer, t + 1))
                    tt(lru_m[:, 0:CW], lru_a[:, 0:CW], lru_a[:, 0:CW], ALU.mult)
                    tt(lru_g[:, 0:CW], lru_g[:, 0:CW], lru_x[:, t, 0:CW], ALU.mult)
                    dve.drain()
                    stt(lru_m[:, 0:CW], lru_m[:, 0:CW], 1.0, lru_u[:, 0:CW], ALU.add, ALU.mult).then_inc(lru_prod.sem, 1)
                    v.memset(lru_a[:, SEQ + 2:STREAM - 1:7], 0.0)
                    dve.wait_ge(lru_root.sem, lru_root.at(layer, t + 1))
                    tt(lru_u[:, 0:CW], lru_m[:, 0:CW], lru_g[:, 0:CW], ALU.mult)
                    dve.drain()
                    copy(lru_u[:, SEQ + 2:STREAM - 1:7], par("lru_h0", 8 * t, 8))
                    dve.drain()
                    v.tensor_tensor_scan(hl[:, t, 0:CW], lru_a[:, 0:CW], lru_u[:, 0:CW], 0.0, ALU.mult, ALU.add)
                    dve.drain()
                    copy(lru_last[:, t, 0:1], hl[:, t, SEQ - 1:SEQ])
                    copy(lru_last[:, t, 1:9].unsqueeze(2), samples(hl[:, t, :], 3, 1)).then_inc(lru_free.sem, 1)

                def gla_gate(_=None):
                    dve.wait_ge(gla_ge.sem, gla_ge.at(layer, 1))
                    stt(tz[:, 0, :], tz[:, 0, :], 0.0, tz[:, 1, :], ALU.min, ALU.subtract)
                    dve.drain()
                    for c, off, n in CH:
                        v.tensor_tensor_scan(gqkc[:, 2, off:off + n], cst("reset_s") if c == SAMPLE else cst("ones"),
                                             tz[:, 0, off:off + n], 0.0, ALU.mult, ALU.add)
                    dve.drain()
                    gla_pre_(0)

                def gla_pre_(c):
                    _, off, n = CH[c]
                    q, k, cum = (gqkc[:, i, off:off + n] for i in range(3))
                    if c < SAMPLE:
                        blocks = cum.rearrange("p (j i) -> p j i", j=4)
                        ref = blocks[:, :, 15:16]
                        tt(D[:], cum.unsqueeze(1).to_broadcast([P, 4, P]), ref.to_broadcast([P, 4, P]), ALU.subtract)
                        tt(ge[:, 0, :].rearrange("p (j i) -> p j i", j=4), ref.to_broadcast([P, 4, 32]), blocks, ALU.subtract)
                        tt(ge[:, 1, :], cum[:, n - 1:n].to_broadcast([P, n]), cum, ALU.subtract)
                        dve.drain()
                        ts(D[:], D[:], CLAMP, None, ALU.min)
                    else:
                        ts(ge[:, 0, 0:n], cum, -1.0, None, ALU.mult)
                        tt(by_sequence(ge[:, 1, 0:n]), by_sequence(cum)[:, :, SLEN - 1:SLEN].to_broadcast([P, NSEQ, SLEN]),
                           by_sequence(cum), ALU.subtract)
                        dve.drain()
                    ts(ge[:, 0, 0:n], ge[:, 0, 0:n], CLAMP, None, ALU.min)
                    copy(ge[:, 2, 0:n], cum)
                    dve.drain().then_inc(gla_diff.sem, 1)
                    dve.wait_ge(gla_exp.sem, gla_exp.at(layer, c + 1))
                    tt(ge[:, 0, 0:n], ge[:, 0, 0:n], k, ALU.mult)
                    if c < SAMPLE:
                        tt(D[:], D[:], q.unsqueeze(1).to_broadcast([P, 4, P]), ALU.mult)
                    tt(ge[:, 1, 0:n], ge[:, 1, 0:n], k, ALU.mult)
                    tt(qt[:, c % 2, 0, 0:n], ge[:, 2, 0:n], q, ALU.mult)
                    dve.drain()
                    tt(kz[:, :, 0:n], ge[:, 0, 0:n].unsqueeze(1).to_broadcast([P, 4, n]),
                       per_head(cst("gla_heads"), P, n), ALU.mult)
                    dve.drain().then_inc(gla_pre.sem, 1)

                def gla_a_(c):
                    _, off, n = CH[c]
                    dve.wait_ge(gla_a.sem, gla_a.at(layer, c + 1))
                    tt(PT[0:n, :, 0:n], M[0][0:n, :].rearrange("p (h i) -> p h i", h=4)[:, :, 0:n],
                       masks(c, "keep").unsqueeze(1).to_broadcast([n, 4, n]), ALU.mult)
                    copy(V[0:n, :], M[1][0:n, 0:256])
                    copy(K[0:n, 0:P], M[1][0:n, 256:384])
                    dve.drain()
                    if c == SAMPLE:
                        dve.wait_ge(stored, layer * STORES + 64)
                        by_seq_values(V)
                        dve.drain()
                    dve.drain().then_inc(gla_bin.sem, 1)
                    if c < SAMPLE:
                        gla_pre_(c + 1)

                def gla_b_(c):
                    dve.wait_ge(gla_b.sem, gla_b.at(layer, c + 1))
                    if c == SAMPLE:
                        dve.wait_ge(s0_loaded.sem, s0_loaded.at(layer, 32))
                        s1 = S1[:, 0:512]
                        tt(s1.rearrange("p (b d) -> p b d", b=NSEQ), S0[:, 0:512].rearrange("p (b d) -> p b d", b=NSEQ),
                           gla_last[:, c % 2, :].unsqueeze(2).to_broadcast([P, NSEQ, 64]), ALU.mult)
                        dve.drain()
                        tt(s1, s1, M[0][:], ALU.add)
                    else:
                        tt((S_gla if c == 0 else dS)[:], M[3][:, 0:256], cst("gla_blocks"), ALU.mult)
                        if c:
                            dve.drain()
                            stt(S_gla[:], S_gla[:], gla_last[:, c % 2, 0:1], dS[:], ALU.mult, ALU.add)
                    dve.drain().then_inc(gla_s.sem, 1)

                def rotate(i):
                    buf = (rk, rk, rq, rq)[i][:, i % 2, :]
                    dve.wait_ge(rot_mm.sem, rot_mm.at(layer, i + 1))
                    for b in range(2):
                        cols = slice(b * HALF, (b + 1) * HALF)
                        tt(sq[:, 0, cols], M[2 + b][:, 0:HALF], cst("sin")[:, cols], ALU.mult)
                    tt(buf, buf, cst("cos"), ALU.mult)
                    dve.drain()
                    tt(buf, buf, sq[:, 0, :], ALU.add)
                    dve.drain().then_inc(rot_out.sem, 1)

                def ret_a_(c):
                    _, off, n = CH[c]
                    dve.wait_ge(ret_a.sem, ret_a.at(layer, c + 1))
                    decay = masks(c, "ret_decay").rearrange("p (t e i) -> p t e i", t=2, e=2)
                    scores = PT[0:n, :, 0:n].rearrange("p (t e) i -> p t e i", e=2)
                    for e in range(2):
                        tt(scores[:, :, e, :], M[e][0:n, 0:256].rearrange("p (t i) -> p t i", t=2)[:, :, 0:n],
                           decay[:, :, e, :], ALU.mult)
                    tt(heads(K[0:n, :]), heads(M[2][0:n, 0:256]), per_head(masks(c, "ret_k"), n, 64), ALU.mult)
                    copy(V[0:n, :], M[2][0:n, 256:512])
                    tt(qt[:, c % 2, :, 0:n], rq[:, :, off:off + n],
                       cst("ret_q_s" if c == SAMPLE else "ret_q").rearrange("p (t i) -> p t i", t=2), ALU.mult)
                    if c == SAMPLE:
                        dve.drain()
                        dve.wait_ge(stored, layer * STORES + 96)
                        by_seq_values(V)
                    dve.drain().then_inc(ret_bin.sem, 1)

                def ret_b_(c):
                    _, off, n = CH[c]
                    dve.wait_ge(ret_b.sem, ret_b.at(layer, c + 1))
                    if c == SAMPLE:
                        for e in range(2):
                            rows = slice(64 * e, 64 * e + 64)
                            copy(rv[rows, :, off:off + n], M[3 - e][rows, 0:2 * n].rearrange("p (t i) -> p t i", t=2))
                        dve.wait_ge(s0_loaded.sem, s0_loaded.at(layer, 48))
                        for t in range(2):
                            cols = slice(512 * t, 512 * t + 512)
                            stt(S1[:, cols], S0[:, cols], cst("ret_last_s")[:, t:t + 1], M[t][:], ALU.mult, ALU.add)
                    else:
                        copy(rv[:, :, off:off + n], M[3][:, 0:256].rearrange("p (t i) -> p t i", t=2))
                        tt((S_ret if c == 0 else dS)[:].rearrange("p (t d) -> p t d", t=2),
                           M[0][:, 0:256].rearrange("p (t d) -> p t d", t=2),
                           cst("ret_blocks").unsqueeze(1).to_broadcast([P, 2, P]), ALU.mult)
                        if c:
                            dve.drain()
                            for t in range(2):
                                cols = slice(P * t, P * t + P)
                                stt(S_ret[:, cols], S_ret[:, cols], cst("ret_last")[:, t:t + 1], dS[:, cols],
                                    ALU.mult, ALU.add)
                    dve.drain().then_inc(ret_s.sem, 1)

                def z_gate(t):
                    dve.wait_ge(gate_act.sem, gate_act.at(layer, t + 1))
                    tt(xbc[:, t, :], xbc[:, t, :], tz[:, t, :], ALU.mult)
                    if t:
                        dve.drain().then_inc(n_in.sem, 1)

                def norm_rstd(i, each, width):
                    dve.wait_ge(n_mm.sem, n_mm.at(layer, i + 1))
                    ts(rstd[:, 0:4 * each], M[4][:, 0:4 * each], 1.0 / width, EPS, ALU.mult, ALU.add)
                    ts(rstd[0:NS, 4 * each:5 * each], M[4][0:NS, 4 * each:5 * each], 1.0 / width, EPS,
                       ALU.mult, ALU.add).then_inc(n_mean.sem, 1)
                    dve.wait_ge(n_root.sem, n_root.at(layer, i + 1))
                    v.reciprocal(rstd[:, 0:5 * each], rstd[:, 0:5 * each]).then_inc(n_rstd.sem, 1)

                def normed(buf, cols, gain, spread):
                    return stt(buf[:, cols], buf[:, cols], gain, spread, ALU.mult, ALU.mult)

                def low(i, g, t, src):
                    dve.wait_ge(y_hi.sem, y_hi.at(layer, i + 1))
                    tt(gl[g][:, t, :], src, gh[g][:, t, :].bitcast(F32), ALU.subtract).then_inc(y_lo.sem, 1)

                prompt, sample = slice(0, SEQ), slice(SEQ, TOK)

                def gla_norm_(i):
                    dve.wait_ge(n_spread.sem, n_spread.at(layer, i + 1))
                    if i < 2:
                        ins = normed(gv[:, i, :], prompt, par("gla_norm", i), M[4][:])
                    else:
                        for t in range(2):
                            ins = normed(gv[:, t, :], sample, par("gla_norm", t), M[4][:, t * NS:(t + 1) * NS])
                    ins.then_inc(n_used.sem, 1)

                def ssd_norm_(i):
                    dve.wait_ge(n_spread.sem, n_spread.at(layer, 4 + i))
                    for t in range(2):
                        ins = normed(xbc[:, t, :], sample if i else prompt, par("ssd_norm", t),
                                     M[4][:, 0:NS] if i else M[4][:])
                    ins.then_inc(n_used.sem, 1)
                    if i:
                        dve.drain().then_inc(y_out.sem, 2)
                        low(0, G_SSD, 0, xbc[:, 0, :])
                        low(1, G_SSD, 1, xbc[:, 1, :])

                def gla_out(t):
                    dve.wait_ge(gate_act.sem, gate_act.at(layer, 5 + t))
                    tt(tz[:, t, :], tz[:, t, :], gv[:, t, :], ALU.mult).then_inc(y_out.sem, 1)
                    low(2 + t, G_GLA, t, tz[:, t, :])

                def lru_out(t):
                    dve.wait_ge(gate_act.sem, gate_act.at(layer, 7 + t))
                    tt(tz[:, t, prompt], tz[:, t, prompt], hl[:, t, prompt], ALU.mult)
                    tt(by_sequence(tz[:, t, sample]), by_sequence(tz[:, t, sample]), samples(hl[:, t, :], 0),
                       ALU.mult).then_inc(y_out.sem, 1)
                    low(4 + t, G_LRU, t, tz[:, t, :])

                def centre(_=None):
                    dve.wait_ge(cent_mm.sem, cent_mm.at(layer, 1))
                    for t in range(2):
                        copy(rv[:, t, prompt], M[t][:])
                        copy(rv[:, t, sample], M[2][:, t * NS:(t + 1) * NS])
                    dve.drain().then_inc(cent_out.sem, 1)

                def ret_norm_(_=None):
                    dve.wait_ge(n_spread.sem, n_spread.at(layer, 6))
                    dve.wait_ge(gate_act.sem, gate_act.at(layer, 4))
                    for t in range(2):
                        normed(rv[:, t, :], prompt, par("ret_norm", t), M[t][:])
                        ins = normed(rv[:, t, :], sample, par("ret_norm", t), M[2][:, t * NS:(t + 1) * NS])
                    ins.then_inc(n_used.sem, 1)
                    dve.drain()
                    for t in range(2):
                        tt(rv[:, t, :], rv[:, t, :], ret_gate[:, t, :], ALU.mult).then_inc(y_out.sem, 1)
                    for t in range(2):
                        low(6 + t, G_RET, t, rv[:, t, :])

                stages = {
                    "dt": dt, "ssd_a": ssd_a_, "ssd_b": ssd_b_, "lru_gates": lru_gates, "gla_gate": gla_gate,
                    "gla_a": gla_a_, "gla_b": gla_b_, "rotate": rotate, "ret_a": ret_a_, "ret_b": ret_b_,
                    "z_gate": z_gate, "gla_stat": lambda: norm_rstd(0, 4, 64), "gla_norm": gla_norm_,
                    "ssd_stat": lambda: norm_rstd(1, 1, 256), "ssd_norm": ssd_norm_, "gla_out": gla_out,
                    "lru_out": lru_out, "centre": centre, "ret_stat": lambda: norm_rstd(2, 4, 64),
                    "ret_norm": ret_norm_,
                }
                for s in range(2 * NIN):
                    evacuate(s // 2, s % 2)
                    for name, *args in SLOTS.get(s, []):
                        stages[name](*args)

                def add_to_h(u, m):
                    for half in range(2):
                        acc, cols = take(u, half)
                        ins = tt(h[:, m, cols], h[:, m, cols], acc, ALU.add)
                        ins.then_inc(dense_free.sem, 1 + (2 * PAD if (u, half) == (NUNIT - 1, 1) else 0))

                def new_h(i, u0, gain):
                    for m in range(KT):
                        add_to_h(u0 + m, m)
                        dve.drain().then_inc(h_new.sem, 1)
                        if m:
                            xl_tile(layer, i, m - 1, par(gain, m - 1))
                    xl_tile(layer, i, KT - 1, par(gain, KT - 1))
                    rms_rstd(layer, i)

                new_h(0, OUT0, "norm_ffn")

                def ffn_pair(j, count, taken):
                    dve.drain()
                    for i in range(4):
                        acc, cols = taken(i)
                        tt(tz[:, i // 2, cols], acc, rs_bcast[:, cols], ALU.mult).then_inc(dense_free.sem, 1)
                        if i == 1:
                            dve.drain().then_inc(gate_out.sem, 1)
                    dve.drain()
                    dve.wait_ge(gate_silu.sem, count)
                    tt(tz[:, 1, :], tz[:, 1, :], tz[:, 0, :], ALU.mult).then_inc(act_out.sem, 1)
                    dve.wait_ge(act_hi.sem, count)
                    hi, lo = operand(j)
                    tt(lo, tz[:, 1, :], hi.bitcast(F32), ALU.subtract).then_inc(act_lo.sem, 1)

                with dve.Fori(0, NGRP) as g:
                    def take_g(i, half):
                        q = 2 * (FFN0 + i) + half
                        dve.wait_ge(dense_done, layer * (2 * LU) + g * (2 * GU) + (q + 1))
                        return dense[q % 3][:, 0:HALF], slice(half * HALF, (half + 1) * HALF)

                    for j in range(GROUP):
                        ffn_pair(j, layer * FT + g * GROUP + (j + 1), lambda i: take_g(2 * j + i // 2, i % 2))
                    for m in range(KT):
                        for half in range(2):
                            acc, cols = take_g(2 * GROUP + m, half)
                            tt(h[:, m, cols], h[:, m, cols], acc, ALU.add).then_inc(dense_free.sem, 1)
                for j in range(REST):
                    ffn_pair(j, layer * FT + (NGRP * GROUP + j + 1), lambda i: take(REST0 + 2 * j + i // 2, i % 2))
                new_h(1, REST0 + 2 * REST, "norm_next")
                dve.drain().then_inc(params_free.sem, 1)

            for m in range(KT):
                stt(h[:, m, :], h[:, m, :], par("norm_next", m), rs_bcast[:], ALU.mult, ALU.mult).then_inc(y_final, 1)

        @block.tensor
        def _(pe):
            mm = nc.tensor.matmul

            def turn(out, src, n_in=P):
                return mm(out, src, cst("ident", n_in, 0, n_in), start=True, stop=True)

            def square_sums(layer, i, m):
                pe.wait_ge(h_squared.sem, h_squared.at(layer, i * KT + m + 1))
                for c, off, n in CH:
                    ins = mm(M[4][0:n, 5 * m + c:5 * m + c + 1], sq[:, m % 2, off:off + n], cst("ones", P, 0, 1),
                             start=True, stop=True)
                ins.then_inc(stat_done.sem, 1)

            def spread_rstd(layer, i):
                pe.wait_ge(rstd_done.sem, rstd_done.at(layer, i + 1))
                for c, off, n in CH:
                    out = M[1][:, 0:n] if c == SAMPLE else M[0][:, off:off + n]
                    ins = mm(out, rstd[0:n, c:c + 1].to_broadcast([n, P]), cst("ident", n, 0, n), start=True, stop=True)
                ins.then_inc(rs_spread.sem, 1)

            pe.wait_ge(in_loaded, 48)
            for m in range(KT):
                square_sums(0, -1, m)
            spread_rstd(0, -1)

            with pe.Fori(0, DEPTH) as layer:

                def half_unit(first, q, slot, n_unit, rhs, ks, before=None, inc=1):
                    pe.wait_ge(dense_free.sem, first)
                    if q % 2 == 0:
                        pe.wait_ge(lo_done, n_unit)
                    cols = slice(q % 2 * HALF, (q % 2 + 1) * HALF)
                    bank_ = dense[q % 3][:, 0:HALF]
                    for i, k in enumerate(ks):
                        if before is not None and q % 2 == 0:
                            before(i)
                        hi, lo = rhs(k)
                        w = slice(i * P, (i + 1) * P)
                        for j, (wt, xx) in enumerate(((wh, hi), (wh, lo), (wl, hi))):
                            ins = mm(bank_, wt[:, slot, w], xx[:, cols], start=(i == 0 and j == 0),
                                     stop=(i == len(ks) - 1 and j == 2))
                    ins.then_inc(dense_done, inc)

                def unit_half(u, half, rhs, ks, before=None):
                    q = 2 * u + half
                    half_unit(layer * (2 * LU) + (q + 1), q, u % RING, layer * LU + (u + 1), rhs, ks, before,
                              1 + (2 * PAD if (u, half) == (NUNIT - 1, 1) else 0))

                def x_operand(k):
                    return xh[:, k, :], xl[:, k, :]

                def dt(_=None):
                    pe.wait_ge(dt_out.sem, dt_out.at(layer, 1))
                    for c, off, n in CH:
                        ins = mm(M[4][0:n, 4 * c:4 * c + 4], misc[32:36, off:off + n], cs[32:36, 32:36],
                                 start=True, stop=True)
                    ins.then_inc(dt_turned.sem, 1)

                def ssd_a_(c):
                    _, off, n = CH[c]
                    if c == 0:
                        pe.wait_ge(dt_ready.sem, dt_ready.at(layer, 1))
                        pe.wait_ge(conv_silu.sem, conv_silu.at(layer, 4))
                    else:
                        pe.wait_ge(ssd_s.sem, ssd_s.at(layer, c))
                    upper = cst("upper_s", n, 0, n) if c == SAMPLE else cst("upper")
                    with_last = cst("upper_s", n) if c == SAMPLE else cst("upper")
                    w = NS + NSEQ if c == SAMPLE else P
                    for r in range(2):
                        for g in range(2):
                            mm(M[1][64 * g:64 * g + 64, r * P:r * P + w],
                               log_a[0:n, c, 2 * g + r:2 * g + r + 1].to_broadcast([n, 64]), with_last,
                               start=True, stop=True)
                    for hd in range(4):
                        mm(M[0][0:n, hd * P:hd * P + n], log_a[0:n, c, hd:hd + 1].to_broadcast([n, n]), upper,
                           start=True, stop=True)
                    mm(M[1][0:n, 256:260], upper, log_a[0:n, c, :], start=True, stop=True)
                    mm(M[1][0:n, 260:264], cst("block_s", n) if c == SAMPLE else cst("ones"), log_a[0:n, c, :],
                       start=True, stop=True)
                    for g in range(2):
                        rows = slice(64 * g, 64 * g + 64)
                        mm(M[2 + g][0:n, 0:n], xbc[rows, 2, off:off + n], xbc[rows, 3, off:off + n], start=True, stop=True)
                    for t in range(3):
                        ins = turn(M[2][0:n, P * (t + 1):P * (t + 2)], xbc[:, t, off:off + n])
                    ins.then_inc(ssd_a.sem, 1)

                def ssd_b_(c):
                    _, off, n = CH[c]
                    pe.wait_ge(ssd_bin.sem, ssd_bin.at(layer, c + 1))
                    if c == SAMPLE:
                        pe.wait_ge(s0_loaded.sem, s0_loaded.at(layer, 16))
                    for hd in range(4):
                        g, r = hd // 2, hd % 2
                        out = M[g][64 * r:64 * r + 64, 0:n]
                        v = V[0:n, 64 * hd:64 * hd + 64]
                        mm(out, v, PT[0:n, hd, 0:n], start=True, stop=c in (0, SAMPLE), skip_group_check=c == SAMPLE)
                        if 0 < c < SAMPLE:
                            mm(out, S_ssd[:, 64 * hd:64 * hd + 64], qt[:, c % 2, r, 0:n], start=False, stop=True)
                    if c < SAMPLE:
                        mm(M[2][:, 0:256], K[0:n, 0:P], Vd[0:n, :], start=True, stop=True).then_inc(ssd_b.sem, 1)
                        return
                    for r in range(2):
                        for g in range(2):
                            rows = slice(64 * g, 64 * g + 64)
                            for b in range(NSEQ):
                                at = (r * NSEQ + b) * 64
                                mm(M[g][64 * r:64 * r + 64, SLEN * b:SLEN * (b + 1)], S0[rows, at:at + 64],
                                   qt[rows, c % 2, r, SLEN * b:SLEN * (b + 1)], start=False, stop=True,
                                   skip_group_check=True)
                    for hd in range(4):
                        g, r = hd // 2, hd % 2
                        ins = mm(M[2 + r][64 * g:64 * g + 64, :], K[0:n, 64 * g:64 * g + 64],
                                 Vx[0:n, 512 * hd:512 * hd + 512], start=True, stop=True)
                    ins.then_inc(ssd_b.sem, 1)

                def lru_gates(t):
                    if t == 0:
                        pe.wait_ge(conv_done.sem, conv_done.at(layer, 6))
                        pe.wait_ge(ssd_s.sem, ssd_s.at(layer, 5))
                    else:
                        pe.wait_ge(lru_sig.sem, lru_sig.at(layer, 1))
                    w = par("lru_w", 0, 512)
                    for i in range(2):
                        for b in range(2):
                            ins = mm(M[2 * i + b][:, 0:CW // 2], w[:, (2 * i + t) * P:(2 * i + t + 1) * P],
                                     lru_x[:, t, b * (CW // 2):(b + 1) * (CW // 2)], start=True, stop=True)
                    ins.then_inc(lru_mm.sem, 1)

                def gla_gate(_=None):
                    pe.wait_ge(lru_sig.sem, lru_sig.at(layer, 2))
                    for b in range(2):
                        ins = mm(M[b][:, 0:HALF], par("gate2", 0, P)[0:16], misc[0:16, b * HALF:(b + 1) * HALF],
                                 start=True, stop=True)
                    ins.then_inc(gla_gmm.sem, 1)

                def gla_a_(c):
                    _, off, n = CH[c]
                    pe.wait_ge(gla_pre.sem, gla_pre.at(layer, c + 1))
                    if c < SAMPLE:
                        for j in range(4):
                            for hd in range(4):
                                mm(M[0][32 * j:32 * j + 32, hd * P:(hd + 1) * P], kz[:, hd, 32 * j:32 * j + 32],
                                   D[:, j, :], start=True, stop=True)
                    else:
                        for hd in range(4):
                            mm(M[0][0:n, hd * P:hd * P + n], kz[:, hd, 0:n], qt[:, c % 2, 0, 0:n], start=True, stop=True)
                    for t in range(2):
                        turn(M[1][0:n, t * P:(t + 1) * P], gv[:, t, off:off + n])
                    turn(M[1][0:n, 256:384], ge[:, 1, 0:n]).then_inc(gla_a.sem, 1)

                def gla_b_(c):
                    _, off, n = CH[c]
                    pe.wait_ge(gla_bin.sem, gla_bin.at(layer, c + 1))
                    if c == 0:
                        pe.wait_ge(rot_out.sem, rot_out.at(layer, 2))
                    else:
                        pe.wait_ge(gla_s.sem, gla_s.at(layer, c))
                        pe.wait_ge(gla_o.sem, gla_o.at(layer, c))
                    if c == SAMPLE:
                        pe.wait_ge(s0_loaded.sem, s0_loaded.at(layer, 32))
                    for hd in range(4):
                        t, e = hd // 2, hd % 2
                        out = (M[2 + t] if c == SAMPLE else M[2])[64 * e:64 * e + 64]
                        out = out[:, 0:n] if c == SAMPLE else out[:, t * P:t * P + n]
                        mm(out, V[0:n, 64 * hd:64 * hd + 64], PT[0:n, hd, 0:n], start=True, stop=c in (0, SAMPLE),
                           skip_group_check=c > 0)
                        if e and 0 < c < SAMPLE:
                            mm(M[2][:, t * P:t * P + n], S_gla[:, t * P:(t + 1) * P], qt[:, c % 2, 0, 0:n],
                               start=False, stop=True, skip_group_check=True)
                    if c < SAMPLE:
                        mm(M[3][:, 0:256], K[0:n, 0:P], V[0:n, :], start=True, stop=True).then_inc(gla_b.sem, 1)
                        return
                    pe.drain()
                    for hd in (0, 2, 1, 3):
                        t, e = hd // 2, hd % 2
                        rows = slice(32 * hd, 32 * hd + 32)
                        for b in range(NSEQ):
                            cols = slice(SLEN * b, SLEN * (b + 1))
                            mm(M[2 + t][64 * e:64 * e + 64, cols], S0[rows, 64 * b:64 * b + 64], qt[rows, c % 2, 0, cols],
                               start=False, stop=True, skip_group_check=True, tile_position=(32 * hd, 64 * e))
                    for hd in range(4):
                        ins = mm(M[0][32 * hd:32 * hd + 32, :], K[0:n, 32 * hd:32 * hd + 32],
                                 Vx[0:n, 512 * hd:512 * hd + 512], start=True, stop=True, tile_position=(0, 32 * hd))
                    ins.then_inc(gla_b.sem, 1)

                def rotate(i):
                    buf = (rk, rk, rq, rq)[i][:, i % 2, :]
                    pe.wait_ge(rot_in.sem, rot_in.at(layer, i + 1))
                    if i == 0:
                        pe.wait_ge(lru_sig.sem, lru_sig.at(layer, 2))
                    elif i == 2:
                        pe.wait_ge(gla_o.sem, gla_o.at(layer, 5))
                    else:
                        pe.wait_ge(rot_out.sem, rot_out.at(layer, i))
                    for b in range(2):
                        ins = mm(M[2 + b][:, 0:HALF], cst("swap"), buf[:, b * HALF:(b + 1) * HALF], start=True, stop=True)
                    ins.then_inc(rot_mm.sem, 1)

                def ret_a_(c):
                    _, off, n = CH[c]
                    if c == 0:
                        pe.wait_ge(rot_out.sem, rot_out.at(layer, 4))
                        pe.wait_ge(gla_s.sem, gla_s.at(layer, 5))
                    else:
                        pe.wait_ge(ret_s.sem, ret_s.at(layer, c))
                    for t in range(2):
                        turn(M[2][0:n, t * P:(t + 1) * P], rk[:, t, off:off + n])
                    for t in range(2):
                        for e in range(2):
                            rows = slice(64 * e, 64 * e + 64)
                            mm(M[e][0:n, t * P:t * P + n], rk[rows, t, off:off + n], rq[rows, t, off:off + n],
                               start=True, stop=True)
                    for t in range(2):
                        ins = turn(M[2][0:n, 256 + t * P:256 + (t + 1) * P], rv[:, t, off:off + n])
                    ins.then_inc(ret_a.sem, 1)

                def ret_b_(c):
                    _, off, n = CH[c]
                    pe.wait_ge(ret_bin.sem, ret_bin.at(layer, c + 1))
                    if c == SAMPLE:
                        pe.wait_ge(s0_loaded.sem, s0_loaded.at(layer, 48))
                    for hd in range(4):
                        t, e = hd // 2, hd % 2
                        out = M[3 - e][64 * e:64 * e + 64, t * n:(t + 1) * n] if c == SAMPLE else \
                            M[3][64 * e:64 * e + 64, t * P:t * P + n]
                        mm(out, V[0:n, 64 * hd:64 * hd + 64], PT[0:n, hd, 0:n], start=True, stop=c in (0, SAMPLE),
                           skip_group_check=c > 0)
                        if e and 0 < c < SAMPLE:
                            mm(M[3][:, t * P:t * P + n], S_ret[:, t * P:(t + 1) * P], qt[:, c % 2, t, 0:n],
                               start=False, stop=True, skip_group_check=True)
                        if c == SAMPLE:
                            rows = slice(64 * e, 64 * e + 64)
                            for b in range(NSEQ):
                                at = (t * NSEQ + b) * 64
                                mm(out[:, SLEN * b:SLEN * (b + 1)], S0[rows, at:at + 64],
                                   qt[rows, c % 2, t, SLEN * b:SLEN * (b + 1)], start=False, stop=True,
                                   skip_group_check=True)
                    if c < SAMPLE:
                        for t in range(2):
                            ins = mm(M[0][:, t * P:(t + 1) * P], K[0:n, t * P:(t + 1) * P], V[0:n, t * P:(t + 1) * P],
                                     start=True, stop=True)
                    else:
                        for hd in range(4):
                            t, e = hd // 2, hd % 2
                            ins = mm(M[t][64 * e:64 * e + 64, :], K[0:n, 64 * hd:64 * hd + 64],
                                     Vx[0:n, 512 * hd:512 * hd + 512], start=True, stop=True)
                    ins.then_inc(ret_b.sem, 1)

                def head_stat(i):
                    pe.wait_ge(n_sq.sem, n_sq.at(layer, i + 1))
                    if i:
                        pe.wait_ge(n_used.sem, n_used.at(layer, 5))
                    for c, off, n in CH:
                        for t in range(2):
                            at = 4 * c + 2 * t
                            ins = mm(M[4][0:n, at:at + 2], sq[:, t, off:off + n], cst("pair"), start=True, stop=True)
                    ins.then_inc(n_mm.sem, 1)

                def head_spread(out, c, t):
                    n = CH[c][2]
                    at = 4 * c + 2 * t
                    for e in range(2):
                        ins = mm(out[64 * e:64 * e + 64], rstd[0:n, at + e:at + e + 1].to_broadcast([n, 64]),
                                 cst("ident", n, 0, n), start=True, stop=True)
                    return ins

                def gla_norm_(i):
                    if i == 0:
                        pe.wait_ge(n_rstd.sem, n_rstd.at(layer, 1))
                    else:
                        pe.wait_ge(n_used.sem, n_used.at(layer, i))
                    if i < 2:
                        for c in range(4):
                            ins = head_spread(M[4][:, c * P:(c + 1) * P], c, i)
                    else:
                        for t in range(2):
                            ins = head_spread(M[4][:, t * NS:(t + 1) * NS], SAMPLE, t)
                    ins.then_inc(n_spread.sem, 1)

                def ssd_stat(_=None):
                    pe.wait_ge(n_sq.sem, n_sq.at(layer, 2))
                    pe.wait_ge(n_used.sem, n_used.at(layer, 3))
                    for c, off, n in CH:
                        for t in range(2):
                            ins = mm(M[4][0:n, c:c + 1], sq[:, t, off:off + n], cst("ones", P, 0, 1),
                                     start=(t == 0), stop=(t == 1))
                    ins.then_inc(n_mm.sem, 1)

                def ssd_norm_(i):
                    if i == 0:
                        pe.wait_ge(n_rstd.sem, n_rstd.at(layer, 2))
                    else:
                        pe.wait_ge(n_used.sem, n_used.at(layer, 4))
                    for c in ([SAMPLE] if i else range(4)):
                        n = CH[c][2]
                        out = M[4][:, 0:n] if i else M[4][:, c * P:(c + 1) * P]
                        ins = mm(out, rstd[0:n, c:c + 1].to_broadcast([n, P]), cst("ident", n, 0, n), start=True, stop=True)
                    ins.then_inc(n_spread.sem, 1)

                def centre(_=None):
                    pe.wait_ge(ret_s.sem, ret_s.at(layer, 5))
                    for t in range(2):
                        mm(M[t][:], cst("centre"), rv[:, t, 0:SEQ], start=True, stop=True)
                        ins = mm(M[2][:, t * NS:(t + 1) * NS], cst("centre"), rv[:, t, SEQ:TOK], start=True, stop=True)
                    ins.then_inc(cent_mm.sem, 1)

                def ret_norm_(_=None):
                    pe.wait_ge(n_rstd.sem, n_rstd.at(layer, 3))
                    for t in range(2):
                        for c in range(4):
                            head_spread(M[t][:, c * P:(c + 1) * P], c, t)
                        ins = head_spread(M[2][:, t * NS:(t + 1) * NS], SAMPLE, t)
                    ins.then_inc(n_spread.sem, 1)

                stages = {
                    "dt": dt, "ssd_a": ssd_a_, "ssd_b": ssd_b_, "lru_gates": lru_gates, "gla_gate": gla_gate,
                    "gla_a": gla_a_, "gla_b": gla_b_, "rotate": rotate, "ret_a": ret_a_, "ret_b": ret_b_,
                    "gla_stat": lambda: head_stat(0), "gla_norm": gla_norm_, "ssd_stat": ssd_stat,
                    "ssd_norm": ssd_norm_, "centre": centre, "ret_stat": lambda: head_stat(2), "ret_norm": ret_norm_,
                }
                for s in range(2 * NIN):
                    def operand_ready(k, s=s):
                        if s == 0:
                            pe.wait_ge(xl_done.sem, xl_done.at(layer, k + 1 - KT))
                    unit_half(s // 2, s % 2, x_operand, range(KT), operand_ready)
                    for name, *args in SLOTS.get(s, []):
                        if name in stages:
                            stages[name](*args)

                for m in range(KT):
                    def result_ready(i, m=m):
                        if m == 0 and i % 2 == 0:
                            pe.wait_ge(y_lo.sem, y_lo.at(layer, i + 2))
                    for half in range(2):
                        unit_half(OUT0 + m, half, operand, OUT_K, result_ready)
                    if m:
                        square_sums(layer, 0, m - 1)

                square_sums(layer, 0, KT - 1)
                spread_rstd(layer, 0)

                with pe.Fori(0, NGRP) as g:
                    for i in range(GU):
                        def ready(k, i=i):
                            if i == 0:
                                pe.wait_ge(xl_done.sem, xl_done.at(layer, k + 1))
                            if i == 2 * GROUP:
                                pe.wait_ge(act_lo.sem, layer * FT + g * GROUP + (k + 1))
                        for half in range(2):
                            q = 2 * (FFN0 + i) + half
                            half_unit(layer * (2 * LU) + g * (2 * GU) + (q + 1), q, i % RING,
                                      layer * LU + g * GU + (FFN0 + i + 1),
                                      x_operand if i < 2 * GROUP else operand, range(KT), ready)
                for i in range(2 * REST + KT):
                    def ready(k, i=i):
                        if i == 2 * REST:
                            pe.wait_ge(act_lo.sem, act_lo.at(layer, NGRP * GROUP + k + 1))
                    for half in range(2):
                        if i < 2 * REST:
                            unit_half(REST0 + i, half, x_operand, range(KT), ready)
                        else:
                            unit_half(REST0 + i, half, operand, range(REST), ready)
                    if i > 2 * REST:
                        square_sums(layer, 1, i - 2 * REST - 1)
                square_sums(layer, 1, KT - 1)
                spread_rstd(layer, 1)



def cut(a):
    a = np.asarray(a)
    return np.moveaxis(a.reshape(a.shape[0] // P, P, *a.shape[1:]), 0, 1)


def constants():
    out = np.zeros((P, NCONST), np.float32)

    def put(name, a):
        a = np.asarray(a, np.float64)
        at, w = CONST[name]
        out[:a.shape[0], at:at + w] = a.reshape(a.shape[0], -1)

    p, q = np.arange(P)[:, None], np.arange(P)[None, :]
    put("ident", p == q)
    put("upper", p <= q)
    put("keep", p <= q)
    put("neg", np.where(p <= q, 0.0, -1e30))
    put("swap", p == q ^ 32)
    put("centre", (p == q) - (p // 64 == q // 64) / 64.0)
    put("ones", np.ones((P, P)))
    wide = np.arange(256)[None, :]
    put("ssd_blocks", p // 64 == wide // 128)
    put("gla_blocks", p // 32 == wide // 64)
    put("ret_blocks", p // 64 == q // 64)
    log_gamma = np.log(1.0 - 2.0 ** (-5.0 - np.arange(4)))
    scale = 64 ** -0.5
    lg = log_gamma[None, :, None]
    put("ret_decay", np.where(p[:, None] <= q[None], scale * np.exp(lg * (q[None] - p[:, None])), 0.0))
    head = 2 * np.arange(2)[None, :] + p // 64
    put("ret_q", np.exp(log_gamma[head][:, :, None] * (np.arange(P) + 1)))
    put("ret_k", scale * np.exp(log_gamma[None] * (P - 1 - p)))
    put("ret_last", np.exp(log_gamma[head] * P))
    put("ret_last_s", np.exp(log_gamma[head] * SLEN))
    j, i = np.arange(NS)[:, None], np.arange(NS)[None, :]
    same = j // SLEN == i // SLEN
    seq = j // SLEN == np.arange(NSEQ)[None, :]
    put("upper_s", np.concatenate([same & (j <= i), seq], axis=1))
    put("neg_s", np.where(same & (j <= i), 0.0, -1e30))
    put("keep_s", same & (j <= i))
    put("block_s", same)
    put("seq_s", seq)
    put("reset_s", np.broadcast_to(i % SLEN != 0, (P, NS)))
    put("ret_decay_s", np.where((same & (j <= i))[:, None], scale * np.exp(lg * (i[None] - j[:, None])), 0.0))
    put("ret_q_s", np.exp(log_gamma[head][:, :, None] * (np.arange(NS) % SLEN + 1)))
    put("ret_k_s", scale * np.exp(log_gamma[None] * (SLEN - 1 - j % SLEN)))
    put("gla_heads", p // GDK == np.arange(4)[None, :])
    put("pair", p // 64 == np.arange(2)[None, :])
    inv = (10000.0 ** (-np.arange(32) / 32.0)).astype(np.float32)
    pos = np.concatenate([np.arange(SEQ), PAST + np.arange(NS) % SLEN]).astype(np.float32)
    ang = (pos[None, :] * inv[:, None]).astype(np.float32).astype(np.float64)
    put("cos", np.tile(np.cos(ang), (4, 1)))
    put("sin", np.tile(np.concatenate([-np.sin(ang), np.sin(ang)]), (2, 1)))
    return out


def pack_weights(w_in, w_out, w_gate, w_up, w_down):
    units = np.zeros((DEPTH * LU + RING, P, KT, P), np.float32)
    lr0, dt0 = 2308, 768
    for d in range(DEPTH):
        out = units[d * LU:(d + 1) * LU]
        for u, (_, c) in enumerate(IN_UNITS):
            if c is None:
                out[u, :, :, 0:16] = cut(w_in[d][:, lr0:lr0 + 16])
                out[u, :, :, 32:36] = cut(w_in[d][:, dt0:dt0 + 4])
            else:
                out[u] = cut(w_in[d][:, c:c + P])
        for m in range(KT):
            out[OUT0 + m] = cut(w_out[d][:, m * P:(m + 1) * P])[:, OUT_K]
        u = FFN0
        for first in range(0, FT, GROUP):
            n = min(GROUP, FT - first)
            for j in range(first, first + n):
                out[u] = cut(w_gate[d][:, j * P:(j + 1) * P])
                out[u + 1] = cut(w_up[d][:, j * P:(j + 1) * P])
                u += 2
            for m in range(KT):
                out[u, :, 0:n] = cut(w_down[d][first * P:(first + n) * P, m * P:(m + 1) * P])
                u += 1
    return units.reshape(DEPTH * LU + RING, P, KT * P)


def pack_params(i):
    out = np.zeros((DEPTH, P, NPARAM), np.float32)
    for d in range(DEPTH):
        def put(name, a):
            at, w = PARAM[name]
            out[d, :a.shape[0], at:at + w] = a.reshape(a.shape[0], -1)

        def taps(w):
            return np.moveaxis(cut(w.T), -1, 2)

        put("norm_ffn", cut(i["norm_ffn"][d]))
        put("norm_next", cut(i["norm_mix"][d + 1] if d + 1 < DEPTH else i["norm_final"]))
        put("ssd_conv_w", taps(i["ssd_conv_w"][d]))
        put("lru_conv_w", taps(i["lru_conv_w"][d]))
        for name in ("ssd_conv_b", "lru_conv_b", "ssd_norm", "ret_norm", "gla_norm", "lru_b_a", "lru_b_x", "lru_lambda"):
            put(name, cut(i[name][d]))
        put("gla_b", cut(i["gla_b_gate"][d]))
        put("ssd_d", cut(np.repeat(i["ssd_d"][d], 64)))
        put("dt_bias", np.broadcast_to(i["ssd_dt_bias"][d], (P, 4)))
        put("a_log", np.broadcast_to(i["ssd_a_log"][d], (P, 4)))
        put("lru_h0", cut(i["state_lru"][d].T))
        history = np.concatenate([i["state_ssd_conv"][d], i["state_lru_conv"][d]], axis=-1)
        put("history", cut(np.transpose(history, (2, 0, 1))))
        w = np.zeros((P, 2, 2, P), np.float32)
        for k, name in enumerate(("lru_w_a", "lru_w_x")):
            for b in range(4):
                r = slice(64 * (b % 2), 64 * (b % 2) + 64)
                w[r, k, b // 2, r] = i[name][d][b]
        put("lru_w", w)
        put("gate2", i["gla_w_gate2"][d])
    return out


def kernel(**inputs):
    import concourse.bacc as bacc
    from concourse.bass_utils import run_bass_kernel_spmd

    i = {k: np.asarray(v) for k, v in inputs.items()}
    x = np.concatenate([i["x_prompt"].reshape(SEQ, DM), i["x_sample"].reshape(NS, DM)]).T
    first_gain = cut(i["norm_mix"][0])
    arrays = {
        "weights": pack_weights(i["w_in"], i["w_out"], i["w_gate"], i["w_up"], i["w_down"]),
        "params": pack_params(i),
        "consts": np.concatenate([constants(), first_gain], axis=1),
        "x": np.ascontiguousarray(cut(x)),
        "s_ssd": i["state_ssd"].reshape(DEPTH, NSEQ, 2, 2, 64, 64).transpose(0, 2, 4, 3, 1, 5).reshape(DEPTH, P, 1024),
        "s_ret": i["state_ret"].reshape(DEPTH, NSEQ, 2, 2, 64, 64).transpose(0, 3, 4, 2, 1, 5).reshape(DEPTH, P, 1024),
        "s_gla": i["state_gla"].transpose(0, 2, 3, 1, 4).reshape(DEPTH, P, 512),
    }
    outs = {"y": (P, KT, TOK), "o_conv": (DEPTH, P, 6, 27), "o_ssd": (DEPTH, P, 256), "o_ret": (DEPTH, P, 256),
            "o_gla": (DEPTH, P, 256), "o_lru": (DEPTH, P, 2, 9), "n_ssd": (DEPTH, P, 1024),
            "n_ret": (DEPTH, P, 1024), "n_gla": (DEPTH, P, 512)}
    nc = bacc.Bacc("TRN2", target_bir_lowering=False, num_devices=1)
    arrays = {k: np.ascontiguousarray(v) for k, v in arrays.items()}
    args = {k: nc.dram_tensor(k, v.shape, F32, kind="ExternalInput").ap() for k, v in arrays.items()}
    args |= {k: nc.dram_tensor(k, shape, F32, kind="ExternalOutput").ap() for k, shape in outs.items()}
    trunk(nc, **args)
    r = run_bass_kernel_spmd(nc, [arrays], core_ids=[0]).results[0]

    y = np.moveaxis(r["y"], 1, 0).reshape(DM, TOK).T
    conv = r["o_conv"].transpose(0, 3, 2, 1).reshape(DEPTH, 27, 6 * P)
    lru = r["o_lru"].transpose(0, 3, 2, 1).reshape(DEPTH, 9, 2 * P)
    conv_p, conv_s = conv[:, None, 0:3], conv[:, 3:].reshape(DEPTH, NSEQ, 3, 6 * P)
    o_ssd = r["o_ssd"].reshape(DEPTH, 2, 64, 2, 2, 64)
    o_ret = r["o_ret"].reshape(DEPTH, 2, 64, 2, 2, 64)
    o_gla = r["o_gla"].reshape(DEPTH, 4, 32, 4, 64)
    p_ssd = np.stack([o_ssd[:, h // 2, :, h // 2, h % 2] for h in range(4)], axis=1)[:, None]
    p_ret = np.stack([o_ret[:, h % 2, :, h // 2, h % 2] for h in range(4)], axis=1)[:, None]
    p_gla = np.stack([o_gla[:, h, :, h] for h in range(4)], axis=1)[:, None]
    s_ssd = r["n_ssd"].reshape(DEPTH, 2, 64, 2, NSEQ, 64).transpose(0, 4, 1, 3, 2, 5).reshape(DEPTH, NSEQ, 4, 64, 64)
    s_ret = r["n_ret"].reshape(DEPTH, 2, 64, 2, NSEQ, 64).transpose(0, 4, 3, 1, 2, 5).reshape(DEPTH, NSEQ, 4, 64, 64)
    s_gla = r["n_gla"].reshape(DEPTH, 4, 32, NSEQ, 64).transpose(0, 3, 1, 2, 4)
    out = (y[:SEQ].reshape(1, SEQ, DM), y[SEQ:].reshape(NSEQ, SLEN, DM),
           conv_p[..., :512], p_ssd, p_ret, p_gla, conv_p[..., 512:], lru[:, 0:1],
           conv_s[..., :512], s_ssd, s_ret, s_gla, conv_s[..., 512:], lru[:, 1:])
    return tuple(np.ascontiguousarray(o) for o in out)
```

```python
from contextlib import ExitStack

import numpy as np

import concourse.bass as bass
from concourse import mybir

ALU = mybir.AluOpType
ACT = mybir.ActivationFunctionType
AX_X = mybir.AxisListType.X
F32 = mybir.dt.float32
F32R = mybir.dt.float32r

P = 128
DM = 1024
KT = DM // P
DEPTH = 2
SEQ = 512
NSEQ = 8
SLEN = 4
NS = NSEQ * SLEN
TOK = SEQ + NS
HALF = TOK // 2
PAST = 4096
EPS = 1e-6
DFF = 2816
FT = DFF // P
CH = [(c, c * P, P) for c in range(SEQ // P)] + [(4, SEQ, NS)]
SAMPLE = 4
GDK = 32
CLAMP = 40.0 * 16.0

STREAM = 3 + SEQ + NSEQ * (3 + SLEN)
CW = STREAM - 3

IN_UNITS = [("misc", None), ("xbc", 256), ("xbc", 384), ("xbc", 512), ("xbc", 640), ("lx", 2836), ("lx", 2964),
            ("gq", 1796), ("gk", 1924), ("gv", 2052), ("gv", 2180), ("rk", 1028), ("rk", 1156),
            ("rq", 772), ("rq", 900), ("rv", 1284), ("rv", 1412), ("z", 0), ("z", 128),
            ("ly", 2580), ("ly", 2708), ("gr", 2324), ("gr", 2452), ("rg", 1540), ("rg", 1668)]
GATE0 = 17
NIN = len(IN_UNITS)
OUT0 = NIN
FFN0 = OUT0 + KT
GROUP = KT
GU = 2 * GROUP + KT
NGRP = FT // GROUP
REST = FT - NGRP * GROUP
REST0 = FFN0 + NGRP * GU
NUNIT = REST0 + 2 * REST + KT
RING = 3
LU = -(-NUNIT // 6) * 6
PAD = LU - NUNIT
assert GU % RING == 0 and (FFN0 % RING, REST0 % RING) == (0, 0)

OUT_K = [0, 1, 6, 7, 4, 5, 2, 3]
G_SSD, G_RET, G_GLA, G_LRU = 0, 1, 2, 3


def columns(widths):
    at, out = 0, {}
    for name, w in widths:
        out[name] = (at, w)
        at += w
    return out, at


CONST, NCONST = columns([
    ("keep", P), ("after", P), ("centre", P), ("ones", 1),
    ("ssd_blocks", 256), ("gla_blocks", 256), ("ret_blocks", P), ("ret_decay", 512), ("ret_q", 256),
    ("cos", TOK), ("sin", TOK), ("keep_s", NS), ("after_s", NS),
    ("seq_s", NSEQ), ("reset_s", NS), ("ret_decay_s", 4 * NS), ("ret_q_s", 2 * NS), ("ret_k", 4), ("ret_k_s", 4),
    ("ret_last", 2), ("ret_last_s", 2), ("gla_heads", 4), ("pair", 2)])

EXACT, NEXACT = columns([("ident", P), ("upper", P), ("minus", P), ("neg", P),
                         ("upper_s", NS + NSEQ), ("minus_s", NS), ("neg_s", NS)])

PARAM, NPARAM = columns([
    ("norm_ffn", 8), ("norm_next", 8), ("ssd_conv_w", 16), ("ssd_conv_b", 4), ("lru_conv_w", 8),
    ("lru_conv_b", 2), ("ssd_d", 2), ("ssd_norm", 2), ("ret_norm", 2), ("gla_norm", 2), ("gla_b", 1),
    ("lru_b_a", 2), ("lru_b_x", 2), ("lru_lambda", 2), ("dt_bias", 4), ("a_log", 4), ("lru_h0", 16),
    ("history", 6 * NSEQ * 3), ("lru_w", 512), ("gate2", P)])

SLOTS = {}


def at_slot(s, name, *args):
    SLOTS.setdefault(s, []).append((name, *args))


at_slot(2, "dt")
at_slot(4, "gla_gate")
at_slot(7, "gla_cum")
for _c in range(5):
    _late = int(_c == 4)
    at_slot(12 + 2 * _c, "ssd_a", _c)
    at_slot(13 + 2 * _c + _late, "ssd_b", _c)
    at_slot(25 + 2 * _c, "gla_a", _c)
    at_slot(26 + 2 * _c, "gla_b", _c)
    at_slot(35 + 2 * _c, "ret_a", _c)
    at_slot(36 + 2 * _c + _late, "ret_b", _c)
at_slot(21, "gla_pre", 0)
for _i in range(2):
    at_slot(23 + _i, "lru_gates", _i)
    at_slot(24 + 2 * _i, "lru_scan", _i)
    at_slot(25 + 4 * _i, "rotate_send", _i)
    at_slot(28 + 4 * _i, "rotate", _i)
    at_slot(36 + 2 * _i, "z_gate", _i)
    at_slot(40 + _i, "ssd_norm", _i)
    at_slot(44 + 2 * _i, "gla_out", _i)
    at_slot(48 + _i, "ret_out", _i)
for _i in range(2):
    at_slot(41 + 2 * _i, "lru_out", _i)
at_slot(34, "gla_squares")
at_slot(35, "gla_stat")
for _i in range(3):
    at_slot(36 + _i, "gla_norm", _i)
at_slot(38, "ssd_squares")
at_slot(39, "ssd_stat")
at_slot(46, "centre")
at_slot(46, "ret_squares")
at_slot(47, "ret_stat")
at_slot(48, "ret_norm")
SLOTS[48].sort(key=lambda stage: stage[0])


class Signal:

    def __init__(self, sem, per_layer, start=0):
        self.sem, self.per_layer, self.start = sem, per_layer, start

    def at(self, layer, n):
        return layer * self.per_layer + (self.start + n)


def trunk(nc, weights, params, consts, x, s_ssd, s_ret, s_gla, y, o_conv, o_ssd, o_ret, o_gla, o_lru,
          n_ssd, n_ret, n_gla):
    with ExitStack() as ctx:
        def sb(name, cols, dt=F32, parts=P):
            return ctx.enter_context(nc.sbuf_tensor(name, [parts, *cols], dt))

        def sem(name):
            return ctx.enter_context(nc.semaphore(name))

        def signal(name, per_layer, start=0):
            return Signal(sem(name), per_layer, start)

        h = sb("h", [KT, TOK])
        xh, xl = sb("xh", [KT, TOK], F32R), sb("xl", [KT, TOK], F32R)
        raw = sb("raw", [RING, KT * P])
        wh, wl = sb("wh", [RING, KT * P], F32R), sb("wl", [RING, KT * P], F32R)
        cs = sb("cs", [NCONST])
        cx = sb("cx", [NEXACT], F32R)
        pr = sb("pr", [NPARAM])
        rs_bcast = sb("rs_bcast", [TOK])
        misc = sb("misc", [TOK], parts=64)
        sp_x, sp_a, sp_e, sp_z = (sb(n, [22]) for n in ("sp_x", "sp_a", "sp_e", "sp_z"))
        sp_2, sp_p, sp_m, sp_y = (sb(n, [22]) for n in ("sp_2", "sp_p", "sp_m", "sp_y"))
        ssd_rate, log_a = sb("ssd_rate", [4]), sb("log_a", [5, 4])
        log_a_hi, log_a_lo = sb("log_a_hi", [5, 4], F32R), sb("log_a_lo", [5, 4], F32R)
        lru_neg, lru_pos = sb("lru_neg", [2]), sb("lru_pos", [2])
        to_last = sb("to_last", [4])
        gla_last = sb("gla_last", [2, NSEQ])
        rstd = sb("rstd", [20])
        rstd_hi, rstd_lo = sb("rstd_hi", [5], F32R), sb("rstd_lo", [5], F32R)
        sq_sum = sb("sq_sum", [TOK])
        PT = sq_sum[:, 0:4 * P].rearrange("p (h i) -> p h i", h=4)
        D = sb("D", [4, P])
        kz = sb("kz", [4, P])
        qt = sb("qt", [2, 2, P])
        E = sb("E", [2, P])
        ge = sb("ge", [3, P])
        V, K, Vd = sb("V", [256]), sb("K", [256]), sb("Vd", [256])
        dS = sb("dS", [256])
        S_ssd, S_gla, S_ret = sb("S_ssd", [256]), sb("S_gla", [256]), sb("S_ret", [256])
        S0 = sb("S0", [1024])
        Vx = sb("Vx", [1024 + 2 * TOK])
        S1 = Vx[:, 0:1024]
        sq = Vx[:, 1024:1024 + 2 * TOK].rearrange("p (t n) -> p t n", t=2)
        gqkc = sb("gqkc", [3, TOK])
        ret_gate = gqkc[:, 0:2, :]
        gv = sb("gv", [2, TOK])
        rq, rk, rv = sb("rq", [2, TOK]), sb("rk", [2, TOK]), sb("rv", [2, TOK])
        hl = sb("hl", [2, STREAM])
        tz = sb("tz", [2, TOK])
        conv_out = sb("conv_out", [6, 27])
        lru_last = sb("lru_last", [2, 1 + NSEQ])

        early = ExitStack()
        xbc = early.enter_context(nc.sbuf_tensor("xbc", [P, 4, TOK], F32))
        early.close()
        gh, gl = [None] * 4, [None] * 4
        gh[G_RET], gl[G_RET] = sb("gh_ret", [2, TOK], F32R), sb("gl_ret", [2, TOK], F32R)
        early = ExitStack()
        cbuf = early.enter_context(nc.sbuf_tensor("cbuf", [P, 3, STREAM], F32))
        ct = early.enter_context(nc.sbuf_tensor("ct", [P, 2, STREAM], F32))
        lru_g, lru_a, lru_m, lru_u = (early.enter_context(nc.sbuf_tensor(n, [P, STREAM], F32))
                                      for n in ("lru_g", "lru_a", "lru_m", "lru_u"))
        lru_x = early.enter_context(nc.sbuf_tensor("lru_x", [P, 2, STREAM], F32))
        early.close()
        for n, i in (("ssd", G_SSD), ("gla", G_GLA), ("lru", G_LRU)):
            gh[i], gl[i] = sb("gh_" + n, [2, TOK], F32R), sb("gl_" + n, [2, TOK], F32R)

        bank = [ctx.enter_context(nc.psum_tensor(f"bank{i}", [P, 512], F32)) for i in range(8)]
        dense, M = bank[0:3], bank[3:8]

        def cst(name, parts=P, lo=0, n=None):
            at, w = CONST[name]
            return cs[0:parts, at + lo:at + (w if n is None else lo + n)]

        def exact(name, parts=P, lo=0, n=None):
            at, w = EXACT[name]
            return cx[0:parts, at + lo:at + (w if n is None else lo + n)]

        def par(name, i=0, n=1):
            at, _ = PARAM[name]
            return pr[:, at + i:at + i + n]

        def masks(c, name):
            return cst(name + "_s" if c == SAMPLE else name, CH[c][2])

        gain_loaded, consts_loaded, exact_loaded = sem("gain_loaded"), sem("consts_loaded"), sem("exact_loaded")
        x_loaded = [sem(f"x_loaded{i}") for i in range(KT // 2)]
        raw_loaded = [sem(f"raw_loaded{i}") for i in range(RING)]
        hi_done, lo_done = sem("hi_done"), sem("lo_done")
        dense_done = sem("dense_done")
        dense_free = Signal(sem("dense_free"), 2 * LU, 3)
        params_free = signal("params_free", 1, 1)
        params_loaded = signal("params_loaded", 16)
        s0_loaded = signal("s0_loaded", 48)
        stored = sem("stored")
        STORES = 8 * 16
        h_new = signal("h_new", 2 * KT)
        h_squared = signal("h_squared", 2 * KT, KT)
        xl_done = signal("xl_done", 2 * KT, KT)
        sq_added = signal("sq_added", 2 * (KT - 1), KT - 1)
        stat_done = signal("stat_done", 2, 1)
        mean_done = signal("mean_done", 2, 1)
        root_done = signal("root_done", 2, 1)
        rstd_done = signal("rstd_done", 2, 1)
        rs_spread = signal("rs_spread", 2, 1)
        gate_out = signal("gate_out", FT)
        gate_silu = signal("gate_silu", FT)
        act_out = signal("act_out", FT)
        act_hi = signal("act_hi", FT)
        act_lo = signal("act_lo", FT)
        dt_out, dt_turned, sp_in, sp_exp = (signal(n, 1) for n in ("dt_out", "dt_turned", "sp_in", "sp_exp"))
        dt_ready = signal("dt_ready", 1)
        conv_done = signal("conv_done", 6)
        conv_silu = signal("conv_silu", 4)
        ssd_a, ssd_e, ssd_dx, ssd_bin, ssd_b, ssd_s = (
            signal(n, 5) for n in ("ssd_a", "ssd_e", "ssd_dx", "ssd_bin", "ssd_b", "ssd_s"))
        lru_mm, lru_sig, lru_prod, lru_root, lru_free = (
            signal(n, 2) for n in ("lru_mm", "lru_sig", "lru_prod", "lru_root", "lru_free"))
        gla_gmm, gla_ge = signal("gla_gmm", 1), signal("gla_ge", 1)
        gla_diff, gla_exp, gla_pre, gla_a, gla_bin, gla_b, gla_s, gla_o = (
            signal(n, 5) for n in ("gla_diff", "gla_exp", "gla_pre", "gla_a", "gla_bin", "gla_b", "gla_s", "gla_o"))
        rot_in, rot_out = signal("rot_in", 4), signal("rot_out", 2)
        rot_sent = signal("rot_sent", 2 * 4 * 16)
        ret_a, ret_bin, ret_b, ret_s = (signal(n, 5) for n in ("ret_a", "ret_bin", "ret_b", "ret_s"))
        gate_in = signal("gate_in", 8)
        gate_act = signal("gate_act", 8)
        y_out = signal("y_out", 8)
        y_hi = signal("y_hi", 8)
        y_lo = signal("y_lo", 8)
        n_in = signal("n_in", 1)
        n_sq, n_mm, n_mean, n_root, n_rstd = (
            signal(n, 3) for n in ("n_sq", "n_mm", "n_mean", "n_root", "n_rstd"))
        n_spread = signal("n_spread", 6)
        n_used = signal("n_used", 6)
        cent_mm, cent_out = signal("cent_mm", 1), signal("cent_out", 1)
        exact_done = sem("exact_done")
        y_final, y_stored = sem("y_final"), sem("y_stored")

        def operand(k):
            return gh[k // 2][:, k % 2, :], gl[k // 2][:, k % 2, :]

        def samples(row, first, n=SLEN):
            return row[:, 3 + SEQ:STREAM].rearrange("p (b l) -> p b l", b=NSEQ)[:, :, first:first + n]

        def by_sequence(cols):
            return cols.rearrange("p (b l) -> p b l", b=NSEQ)

        block = ctx.enter_context(nc.Block())

        @block.sync
        def _(sp):
            sp.dma_start(raw[:, 0, :], weights[0]).then_inc(raw_loaded[0], 16)
            sp.wait_ge(x_loaded[1], 16)
            sp.dma_start(raw[:, 1, :], weights[1]).then_inc(raw_loaded[1], 16)
            sp.wait_ge(x_loaded[KT // 2 - 1], 16)
            sp.dma_start(S1[:, 0:NEXACT], consts[:, NCONST + KT:NCONST + KT + NEXACT]).then_inc(exact_loaded, 16)
            sp.dma_start(cs[:], consts[:, 0:NCONST]).then_inc(consts_loaded, 16)
            sp.dma_start(raw[:, 2, :], weights[2]).then_inc(raw_loaded[2], 16)
            with sp.Fori(0, DEPTH * LU // RING) as turn:
                for s in range(RING):
                    sp.wait_ge(lo_done, turn * RING + (s + 1))
                    sp.dma_start(raw[:, s, :], weights[turn * RING + (s + RING)]).then_inc(raw_loaded[s], 16)
            for s in range(RING):
                sp.wait_ge(raw_loaded[s], 16 * (DEPTH * LU // RING + 1))
            for i in range(KT // 2):
                sp.wait_ge(y_final, 2 * i + 2)
                sp.dma_start(y[:, 2 * i:2 * i + 2, :], h[:, 2 * i:2 * i + 2, :]).then_inc(y_stored, 16)
            sp.wait_ge(y_stored, 16 * (KT // 2))
            sp.wait_ge(stored, DEPTH * STORES)

        @block.gpsimd
        def _(pool):
            def split(s, n):
                pool.wait_ge(hi_done, n + 1)
                nc.gpsimd.tensor_tensor(wl[:, s, :], raw[:, s, :], wh[:, s, :].bitcast(F32),
                                        ALU.subtract).then_inc(lo_done, 1)

            for s in range(RING):
                split(s, s)
            with pool.Fori(0, DEPTH * LU // RING) as turn:
                for s in range(RING):
                    split(s, turn * RING + (s + RING))

        @block.scalar
        def _(act):
            a = nc.scalar.activation

            def hi_first(s):
                act.wait_ge(raw_loaded[s], 16)
                a(wh[:, s, :], raw[:, s, :], ACT.Copy).then_inc(hi_done, 1)

            def hi_ahead(layer, u):
                s = u % RING
                act.wait_ge(raw_loaded[s], layer * (16 * LU // RING) + 16 * (u // RING + 2))
                act.wait_ge(dense_done, layer * (2 * LU) + 2 * (u + 1))
                a(wh[:, s, :], raw[:, s, :], ACT.Copy).then_inc(hi_done, 1)

            def hi_ahead_group(layer, g, i):
                s = i % RING
                act.wait_ge(raw_loaded[s], layer * (16 * LU // RING) + g * (16 * GU // RING)
                            + 16 * ((FFN0 + i) // RING + 2))
                act.wait_ge(dense_done, layer * (2 * LU) + g * (2 * GU) + 2 * (FFN0 + i + 1))
                a(wh[:, s, :], raw[:, s, :], ACT.Copy).then_inc(hi_done, 1)

            def next_operand(layer, i, m, gain):
                act.wait_ge(h_new.sem, h_new.at(layer, i * KT + m + 1))
                if m >= 3:
                    act.wait_ge(sq_added.sem, sq_added.at(layer, i * (KT - 1) + m - 2))
                a(sq[:, m % 2, :] if m else sq_sum[:], h[:, m, :], ACT.Square)
                a(xh[:, m, :], h[:, m, :], ACT.Copy, scale=gain(m)).then_inc(h_squared.sem, 1)

            def root(layer, i):
                act.wait_ge(mean_done.sem, mean_done.at(layer, i + 1))
                a(rstd[:, 0:5], rstd[:, 0:5], ACT.Sqrt).then_inc(root_done.sem, 1)

            act.dma_start(tz[:, 0, 0:KT], consts[:, NCONST:NCONST + KT]).then_inc(gain_loaded, 16)
            for i in range(KT // 2):
                act.dma_start(h[:, 2 * i:2 * i + 2, :], x[:, 2 * i:2 * i + 2, :]).then_inc(x_loaded[i], 16)
            hi_first(0)
            act.wait_ge(gain_loaded, 16)
            for m in range(KT):
                act.wait_ge(x_loaded[m // 2], 16)
                if m >= 3:
                    act.wait_ge(sq_added.sem, m - 2)
                a(xh[:, m, :], h[:, m, :], ACT.Copy, scale=tz[:, 0, m:m + 1])
                a(sq[:, m % 2, :] if m else sq_sum[:], h[:, m, :], ACT.Square).then_inc(h_squared.sem, 1)
            for s in range(1, RING):
                hi_first(s)
            act.wait_ge(mean_done.sem, 1)
            a(rstd[:, 0:5], rstd[:, 0:5], ACT.Sqrt).then_inc(root_done.sem, 1)

            with act.Fori(0, DEPTH) as layer:
                act.wait_ge(params_free.sem, params_free.at(layer, 0))
                act.dma_start(pr[:], params[layer]).then_inc(params_loaded.sem, 16)
                act.dma_start(S0[:], s_ssd[layer]).then_inc(s0_loaded.sem, 16)

                def dt(_=None):
                    act.wait_ge(params_loaded.sem, params_loaded.at(layer, 16))
                    a(ssd_rate[:], par("a_log", 0, 4), ACT.Exp)
                    act.wait_ge(sp_in.sem, sp_in.at(layer, 1))
                    a(sp_a[:], sp_x[:], ACT.Abs)
                    act.drain()
                    a(sp_e[:], sp_a[:], ACT.Exp, scale=-1.0).then_inc(sp_exp.sem, 1)

                def silu_conv(t):
                    act.wait_ge(conv_done.sem, conv_done.at(layer, t + 1))
                    a(xbc[:, t, 0:SEQ], ct[:, t % 2, 0:SEQ], ACT.Silu)
                    a(by_sequence(xbc[:, t, SEQ:TOK]), samples(ct[:, t % 2, :], 0), ACT.Silu).then_inc(conv_silu.sem, 1)

                def ssd_a_(c):
                    n = CH[c][2]
                    w = NS + NSEQ if c == SAMPLE else P
                    act.wait_ge(ssd_a.sem, ssd_a.at(layer, c + 1))
                    a(E[:, :, 0:w], M[1][:, 0:256].rearrange("p (r i) -> p r i", r=2)[:, :, 0:w],
                      ACT.Exp)
                    a(to_last[0:n, :], M[1][0:n, 256:260], ACT.Exp).then_inc(ssd_e.sem, 1)
                    a(D[0:n, :, 0:n], M[0][0:n, :].rearrange("p (h i) -> p h i", h=4)[:, :, 0:n],
                      ACT.Exp).then_inc(ssd_dx.sem, 1)

                def lru_gates(t):
                    act.wait_ge(lru_mm.sem, lru_mm.at(layer, t + 1))
                    if t:
                        act.wait_ge(lru_free.sem, lru_free.at(layer, t))
                    for b in range(2):
                        a(lru_m[:, b * (CW // 2):(b + 1) * (CW // 2)], M[b][:, 0:CW // 2], ACT.Sigmoid,
                          bias=par("lru_b_a", t))
                    for b in range(2):
                        a(lru_g[:, b * (CW // 2):(b + 1) * (CW // 2)], M[2 + b][:, 0:CW // 2], ACT.Sigmoid,
                          bias=par("lru_b_x", t))
                    act.drain()
                    a(lru_a[:, 0:CW], lru_m[:, 0:CW], ACT.Exp, scale=lru_neg[:, t:t + 1])
                    a(lru_u[:, 0:CW], lru_m[:, 0:CW], ACT.Tanh, scale=lru_pos[:, t:t + 1]).then_inc(lru_sig.sem, 1)

                def lru_scan(t):
                    act.wait_ge(lru_prod.sem, lru_prod.at(layer, t + 1))
                    a(lru_m[:, 0:CW], lru_m[:, 0:CW], ACT.Sqrt).then_inc(lru_root.sem, 1)

                def gla_gate(_=None):
                    act.wait_ge(gla_gmm.sem, gla_gmm.at(layer, 1))
                    for b in range(2):
                        a(tz[:, 0, b * HALF:(b + 1) * HALF], M[b][:, 0:HALF], ACT.Identity, bias=par("gla_b"))
                    act.drain()
                    a(tz[:, 1, :], tz[:, 0, :], ACT.Abs)
                    act.drain()
                    a(tz[:, 1, :], tz[:, 1, :], ACT.Exp, scale=-1.0)
                    act.drain()
                    a(tz[:, 1, :], tz[:, 1, :], ACT.Ln, bias=1.0).then_inc(gla_ge.sem, 1)

                def gla_pre_(c):
                    n = CH[c][2]
                    act.wait_ge(gla_diff.sem, gla_diff.at(layer, c + 1))
                    s = 1.0 / 16.0
                    if c < SAMPLE:
                        a(D[:], D[:], ACT.Exp, scale=s)
                        a(gla_last[:, c % 2, 0:1], gqkc[:, 2, CH[c][1] + P - 1:CH[c][1] + P], ACT.Exp, scale=s)
                    else:
                        a(gla_last[:, c % 2, :], gqkc[:, 2, SEQ + SLEN - 1:TOK:SLEN], ACT.Exp, scale=s)
                    a(ge[:, :, 0:n], ge[:, :, 0:n], ACT.Exp, scale=s).then_inc(gla_exp.sem, 1)

                def gla_b_(c):
                    _, off, n = CH[c]
                    act.wait_ge(gla_b.sem, gla_b.at(layer, c + 1))
                    for t in range(2):
                        src = M[2][:, t * P:t * P + n] if c < SAMPLE else M[2 + t][:, 0:n]
                        ins = a(gv[:, t, off:off + n], src, ACT.Copy)
                    ins.then_inc(gla_o.sem, 1)

                def gate(i, func):
                    act.wait_ge(gate_in.sem, gate_in.at(layer, i + 1))
                    buf = ret_gate if i >= 6 else tz
                    a(buf[:, i % 2, :], buf[:, i % 2, :], func).then_inc(gate_act.sem, 1)

                def norm_root(i, n):
                    act.wait_ge(n_mean.sem, n_mean.at(layer, i + 1))
                    a(rstd[:, 0:n], rstd[:, 0:n], ACT.Sqrt).then_inc(n_root.sem, 1)

                def squares(src):
                    a(sq, src, ACT.Square).then_inc(n_sq.sem, 1)

                def high(i, g, t, src):
                    act.wait_ge(y_out.sem, y_out.at(layer, i + 1))
                    a(gh[g][:, t, :], src, ACT.Copy).then_inc(y_hi.sem, 1)

                def gla_squares(_=None):
                    act.drain()
                    act.wait_ge(rot_out.sem, rot_out.at(layer, 2))
                    squares(gv[:])

                def ssd_squares(_=None):
                    act.wait_ge(n_in.sem, n_in.at(layer, 1))
                    squares(xbc[:, 0:2, :])

                def ssd_norm(i):
                    if i == 1:
                        high(0, G_SSD, 0, xbc[:, 0, :])
                        high(1, G_SSD, 1, xbc[:, 1, :])

                def ret_squares(_=None):
                    act.wait_ge(cent_out.sem, cent_out.at(layer, 1))
                    squares(rv[:])

                def rotate_send(i):
                    act.wait_ge(rot_in.sem, rot_in.at(layer, 2 * i + 2))
                    for q in range(4):
                        to, of = slice(32 * q, 32 * q + 32), slice(32 * (q ^ 1), 32 * (q ^ 1) + 32)
                        act.dma_start((sq if i else rv)[to], (rq if i else rk)[of]).then_inc(rot_sent.sem, 16)

                stages = {
                    "dt": dt, "ssd_a": ssd_a_, "lru_gates": lru_gates, "gla_gate": gla_gate, "gla_b": gla_b_,
                    "lru_scan": lru_scan, "gla_squares": gla_squares, "gla_stat": lambda: norm_root(0, 20),
                    "ssd_squares": ssd_squares, "ssd_stat": lambda: norm_root(1, 5), "ssd_norm": ssd_norm,
                    "lru_out": lambda t: high(2 + t, G_LRU, t, tz[:, t, :]),
                    "gla_out": lambda t: high(4 + t, G_GLA, t, tz[:, t, :]),
                    "ret_out": lambda t: high(6 + t, G_RET, t, rv[:, t, :]),
                    "ret_squares": ret_squares, "ret_stat": lambda: norm_root(2, 20), "rotate_send": rotate_send, "gla_pre": gla_pre_,
                }

                for s in range(2 * NIN):
                    u = s // 2
                    if s % 2:
                        name = IN_UNITS[u][0]
                        if u < NIN - 1:
                            hi_ahead(layer, u)
                        if name == "xbc":
                            silu_conv(u - 1)
                        if name in ("z", "rg", "gr", "ly"):
                            gate(u - GATE0, ACT.Gelu_apprx_tanh if name == "ly" else ACT.Silu)
                    for name, *args in SLOTS.get(s, []):
                        if name in stages:
                            stages[name](*args)
                        if (name, *args) == ("ssd_b", SAMPLE):
                            act.wait_ge(ssd_s.sem, ssd_s.at(layer, 5))
                            act.dma_start(o_ssd[layer], S_ssd[:]).then_inc(stored, 16)
                            act.dma_start(n_ssd[layer], S1).then_inc(stored, 16)
                            act.dma_start(o_conv[layer], conv_out[:]).then_inc(stored, 16)
                            act.dma_start(S0[:, 0:512], s_gla[layer]).then_inc(s0_loaded.sem, 16)
                        if (name, *args) == ("gla_a", 1):
                            act.wait_ge(lru_free.sem, lru_free.at(layer, 2))
                            act.dma_start(o_lru[layer], lru_last[:]).then_inc(stored, 16)
                        if name == "gla_a" and args[0] < SAMPLE:
                            gla_pre_(args[0] + 1)
                        if (name, *args) == ("gla_b", SAMPLE):
                            act.wait_ge(gla_s.sem, gla_s.at(layer, 5))
                            act.dma_start(o_gla[layer], S_gla[:]).then_inc(stored, 16)
                            act.dma_start(n_gla[layer], S1[:, 0:512]).then_inc(stored, 16)
                            act.dma_start(S0[:], s_ret[layer]).then_inc(s0_loaded.sem, 16)
                        if (name, *args) == ("ret_b", SAMPLE):
                            act.wait_ge(ret_s.sem, ret_s.at(layer, 5))
                            act.dma_start(o_ret[layer], S_ret[:]).then_inc(stored, 16)
                            act.dma_start(n_ret[layer], S1).then_inc(stored, 16)

                hi_ahead(layer, NIN - 1)

                for m in range(KT):
                    hi_ahead(layer, OUT0 + m)
                    next_operand(layer, 0, m, lambda m: par("norm_ffn", m))
                root(layer, 0)

                def ffn_unit(i, count):
                    if i % 2 == 0:
                        act.wait_ge(gate_out.sem, count)
                        a(tz[:, 0, :], tz[:, 0, :], ACT.Silu).then_inc(gate_silu.sem, 1)
                    else:
                        act.wait_ge(act_out.sem, count)
                        a(operand(i // 2)[0], tz[:, 1, :], ACT.Copy).then_inc(act_hi.sem, 1)

                with act.Fori(0, NGRP) as g:
                    for i in range(GU):
                        hi_ahead_group(layer, g, i)
                        if i < 2 * GROUP:
                            ffn_unit(i, layer * FT + g * GROUP + (i // 2 + 1))
                for i in range(2 * REST + KT):
                    hi_ahead(layer, REST0 + i)
                    if i < 2 * REST:
                        ffn_unit(i, layer * FT + (NGRP * GROUP + i // 2 + 1))
                    if i >= 2 * REST:
                        next_operand(layer, 1, i - 2 * REST, lambda m: par("norm_next", m))
                for i in range(PAD):
                    hi_ahead(layer, NUNIT + i)
                root(layer, 1)
                act.wait_ge(stored, (layer + 1) * STORES)

        @block.vector
        def _(dve):
            v = nc.vector
            tt, ts, stt, copy = v.tensor_tensor, v.tensor_scalar, v.scalar_tensor_tensor, v.tensor_copy

            def bc(ap, *shape):
                return ap.to_broadcast([ap.shape[0], *shape])

            def split_rstd():
                dve.drain()
                copy(rstd_hi[:], rstd[:, 0:5])
                dve.drain()
                return tt(rstd_lo[:], rstd[:, 0:5], rstd_hi[:].bitcast(F32), ALU.subtract)

            def rms_rstd(layer, i):
                dve.wait_ge(stat_done.sem, stat_done.at(layer, i + 1))
                ts(rstd[:, 0:4], M[4][:, 0:4], 1.0 / DM, EPS, ALU.mult, ALU.add)
                ts(rstd[0:NS, 4:5], M[4][0:NS, 4:5], 1.0 / DM, EPS, ALU.mult, ALU.add).then_inc(mean_done.sem, 1)
                dve.wait_ge(root_done.sem, root_done.at(layer, i + 1))
                v.reciprocal(rstd[:, 0:5], rstd[:, 0:5])
                split_rstd().then_inc(rstd_done.sem, 1)
                dve.wait_ge(rs_spread.sem, rs_spread.at(layer, i + 1))
                copy(rs_bcast[:, 0:SEQ], M[0][:])
                copy(rs_bcast[:, SEQ:TOK], M[1][:, 0:NS])
                dve.drain()

            def xl_tile(layer, i, m, gain):
                dve.wait_ge(h_squared.sem, h_squared.at(layer, i * KT + m + 1))
                stt(xl[:, m, :], h[:, m, :], gain, xh[:, m, :].bitcast(F32), ALU.mult,
                    ALU.subtract).then_inc(xl_done.sem, 1)
                if m:
                    dve.drain()
                    tt(sq_sum[:], sq_sum[:], sq[:, m % 2, :], ALU.add).then_inc(sq_added.sem, 1)

            v.memset(sp_x[:], 0.0).then_inc(dense_free.sem, 3)
            v.memset(rstd[:], 1.0)
            dve.drain().then_inc(params_free.sem, 1)
            for m in range(KT):
                xl_tile(0, -1, m, tz[:, 0, m:m + 1])
            dve.wait_ge(exact_loaded, 16)
            copy(cx[:], S1[:, 0:NEXACT]).then_inc(exact_done, 1)
            dve.wait_ge(consts_loaded, 16)
            rms_rstd(0, -1)

            with dve.Fori(0, DEPTH) as layer:

                def take(u, half):
                    q = 2 * u + half
                    dve.wait_ge(dense_done, layer * (2 * LU) + (q + 1))
                    return dense[q % 3][:, 0:HALF], slice(half * HALF, (half + 1) * HALF)

                def conv(t, half):
                    u, slot = 1 + t, t % 3
                    acc, cols = take(u, half)
                    row = cbuf[:, slot, :]
                    if half == 0:
                        if t == 0:
                            dve.wait_ge(params_loaded.sem, params_loaded.at(layer, 16))
                        v.memset(row[:, 0:3], 0.0)
                        copy(samples(row, 0, 3), par("history", t * 24, 24).rearrange("p (b l) -> p b l", b=NSEQ))
                        tt(row[:, 3:3 + HALF], acc, rs_bcast[:, cols], ALU.mult).then_inc(dense_free.sem, 1)
                        return
                    n = SEQ - HALF
                    tt(row[:, 3 + HALF:3 + SEQ], acc[:, 0:n], rs_bcast[:, HALF:SEQ], ALU.mult)
                    tt(samples(row, 3), by_sequence(acc[:, n:HALF]), by_sequence(rs_bcast[:, SEQ:TOK]),
                       ALU.mult).then_inc(dense_free.sem, 1)
                    dve.drain()
                    copy(conv_out[:, t, 0:3], row[:, SEQ:SEQ + 3])
                    copy(conv_out[:, t, 3:27].rearrange("p (b l) -> p b l", b=NSEQ), samples(row, 4, 3))
                    w, b = ("ssd_conv_w", par("ssd_conv_b", t)) if t < 4 else ("lru_conv_w", par("lru_conv_b", t - 4))
                    out = (ct[:, t % 2, :] if t < 4 else lru_x[:, t - 4, :])[:, 0:CW]
                    if 2 <= t < 4:
                        dve.wait_ge(conv_silu.sem, conv_silu.at(layer, t - 1))
                    ts(out, row[:, 0:CW], par(w, 4 * (t % 4)), b, ALU.mult, ALU.add)
                    for j in range(1, 4):
                        dve.drain()
                        ins = stt(out, row[:, j:j + CW], par(w, 4 * (t % 4) + j), out, ALU.mult, ALU.add)
                    ins.then_inc(conv_done.sem, 1)

                def evacuate(u, half):
                    name = IN_UNITS[u][0]
                    if name in ("xbc", "lx"):
                        return conv(u - 1, half)
                    if half == 0 and name in ("z", "gr", "ly"):
                        dve.drain()
                    acc, cols = take(u, half)
                    if name == "misc":
                        ins = tt(misc[:, cols], acc[0:64], rs_bcast[0:64, cols], ALU.mult)
                        ins.then_inc(dense_free.sem, 1)
                        if half:
                            dve.drain().then_inc(dt_out.sem, 1)
                        return
                    if name == "gq":
                        stt(gqkc[:, 0, cols], acc, GDK ** -0.5, rs_bcast[:, cols], ALU.mult,
                            ALU.mult).then_inc(dense_free.sem, 1)
                        return
                    first = [n for n, _ in IN_UNITS].index(name)
                    dst = {"gk": gqkc[:, 1:2, :], "gv": gv, "rk": rk, "rq": rq, "rv": rv, "z": tz, "rg": ret_gate,
                           "gr": tz, "ly": tz}[name][:, u - first, cols]
                    tt(dst, acc, rs_bcast[:, cols], ALU.mult).then_inc(dense_free.sem, 1)
                    if half and name in ("rk", "rq"):
                        dve.drain().then_inc(rot_in.sem, 1)
                    if half and name in ("z", "rg", "gr", "ly"):
                        dve.drain().then_inc(gate_in.sem, 1)

                def by_seq_values(src):
                    tt(Vx[0:NS, 0:2048].rearrange("p (h b d) -> p h b d", h=4, b=NSEQ),
                       src[0:NS, :].rearrange("p (h d) -> p h d", h=4).unsqueeze(2).to_broadcast([NS, 4, NSEQ, 64]),
                       cst("seq_s", NS).unsqueeze(1).unsqueeze(3).to_broadcast([NS, 4, NSEQ, 64]), ALU.mult)

                def heads(ap):
                    return ap.rearrange("p (h d) -> p h d", h=4)

                def per_head(ap4, n, d):
                    return ap4.unsqueeze(2).to_broadcast([n, 4, d])

                def dt(_=None):
                    dve.wait_ge(dt_turned.sem, dt_turned.at(layer, 1))
                    bias = par("dt_bias", 0, 4)
                    tt(sp_x[:, 0:16].rearrange("p (c h) -> p c h", h=4), M[4][:, 0:16].rearrange("p (c h) -> p c h", h=4),
                       bias.unsqueeze(1).to_broadcast([P, 4, 4]), ALU.add)
                    tt(sp_x[0:NS, 16:20], M[4][0:NS, 16:20], bias[0:NS], ALU.add)
                    ts(sp_x[:, 20:22], par("lru_lambda", 0, 2), -1.0, None, ALU.mult)
                    dve.drain().then_inc(sp_in.sem, 1)
                    ts(sp_m[:], sp_x[:], 0.0, None, ALU.max)
                    dve.wait_ge(sp_exp.sem, sp_exp.at(layer, 1))
                    ts(sp_z[:], sp_e[:], 2.0, None, ALU.add)
                    dve.drain()
                    v.reciprocal(sp_z[:], sp_z[:])
                    dve.drain()
                    tt(sp_z[:], sp_z[:], sp_e[:], ALU.mult)
                    dve.drain()
                    tt(sp_2[:], sp_z[:], sp_z[:], ALU.mult)
                    dve.drain()
                    ts(sp_p[:], sp_2[:], 1.0 / 15.0, None, ALU.mult)
                    for k in (13, 11, 9, 7, 5, 3):
                        dve.drain()
                        stt(sp_p[:], sp_p[:], 1.0 / k, sp_2[:], ALU.add, ALU.mult)
                    dve.drain()
                    stt(sp_p[:], sp_p[:], 1.0, sp_z[:], ALU.add, ALU.mult)
                    dve.drain()
                    stt(sp_y[:], sp_p[:], 2.0, sp_m[:], ALU.mult, ALU.add)
                    dve.drain()
                    stt(log_a[:], sp_y[:, 0:20].rearrange("p (c h) -> p c h", h=4), -1.0,
                        ssd_rate[:].unsqueeze(1).to_broadcast([P, 5, 4]), ALU.mult, ALU.mult)
                    dve.drain()
                    copy(log_a_hi[:], log_a[:])
                    dve.drain()
                    tt(log_a_lo[:], log_a[:], log_a_hi[:].bitcast(F32), ALU.subtract)
                    ts(lru_neg[:], sp_y[:, 20:22], -8.0, None, ALU.mult)
                    ts(lru_pos[:], sp_y[:, 20:22], 8.0, None, ALU.mult)
                    dve.drain().then_inc(dt_ready.sem, 1)

                def ssd_a_(c):
                    _, off, n = CH[c]
                    dve.wait_ge(ssd_a.sem, ssd_a.at(layer, c + 1))
                    tt(heads(V[0:n, :]), heads(M[2][0:n, 128:384]), per_head(sp_y[0:n, 4 * c:4 * c + 4], n, 64), ALU.mult)
                    copy(K[0:n, 0:P], M[2][0:n, 384:512])
                    dve.wait_ge(ssd_e.sem, ssd_e.at(layer, c + 1))
                    tt(qt[:, c % 2, :, 0:n], E[:, :, 0:n], xbc[:, 3, off:off + n].unsqueeze(1).to_broadcast([P, 2, n]),
                       ALU.mult)
                    dve.drain()
                    tt(heads(Vd[0:n, :]), heads(V[0:n, :]), per_head(to_last[0:n, :], n, 64), ALU.mult)
                    if c == SAMPLE:
                        dve.drain()
                        by_seq_values(Vd)
                    dve.wait_ge(ssd_dx.sem, ssd_dx.at(layer, c + 1))
                    for g in range(2):
                        tt(PT[0:n, 2 * g:2 * g + 2, 0:n], D[0:n, 2 * g:2 * g + 2, 0:n],
                           M[2 + g][0:n, 0:n].unsqueeze(1).to_broadcast([n, 2, n]), ALU.mult)
                    dve.drain().then_inc(ssd_bin.sem, 1)

                def ssd_b_(c):
                    _, off, n = CH[c]
                    dve.wait_ge(ssd_b.sem, ssd_b.at(layer, c + 1))
                    for g in range(2):
                        xs = xbc[:, g, off:off + n]
                        stt(xs, xs, par("ssd_d", g), M[g][:, 0:n], ALU.mult, ALU.add)
                    if c == SAMPLE:
                        dve.wait_ge(s0_loaded.sem, s0_loaded.at(layer, 16))
                        tt(S1.rearrange("p (r b d) -> p r b d", r=2, b=NSEQ),
                           S0[:].rearrange("p (r b d) -> p r b d", r=2, b=NSEQ),
                           E[:, :, NS:NS + NSEQ].unsqueeze(3).to_broadcast([P, 2, NSEQ, 64]), ALU.mult)
                        dve.drain()
                        for r in range(2):
                            tt(S1[:, 512 * r:512 * r + 512], S1[:, 512 * r:512 * r + 512], M[2 + r][:], ALU.add)
                    else:
                        tt((S_ssd if c == 0 else dS)[:], M[2][:, 0:256], cst("ssd_blocks"), ALU.mult)
                        if c:
                            dve.drain()
                            for r in range(2):
                                new, old = (x[:].rearrange("p (g r d) -> p g r d", g=2, r=2)[:, :, r, :] for x in (dS, S_ssd))
                                stt(old, old, E[:, r, P - 1:P], new, ALU.mult, ALU.add)
                    dve.drain().then_inc(ssd_s.sem, 1)

                def lru_scan(t):
                    dve.wait_ge(lru_sig.sem, lru_sig.at(layer, t + 1))
                    tt(lru_m[:, 0:CW], lru_a[:, 0:CW], lru_a[:, 0:CW], ALU.mult)
                    tt(lru_g[:, 0:CW], lru_g[:, 0:CW], lru_x[:, t, 0:CW], ALU.mult)
                    dve.drain()
                    stt(lru_m[:, 0:CW], lru_m[:, 0:CW], 1.0, lru_u[:, 0:CW], ALU.add, ALU.mult).then_inc(lru_prod.sem, 1)
                    v.memset(lru_a[:, SEQ + 2:STREAM - 1:7], 0.0)
                    dve.wait_ge(lru_root.sem, lru_root.at(layer, t + 1))
                    tt(lru_u[:, 0:CW], lru_m[:, 0:CW], lru_g[:, 0:CW], ALU.mult)
                    dve.drain()
                    copy(lru_u[:, SEQ + 2:STREAM - 1:7], par("lru_h0", 8 * t, 8))
                    dve.drain()
                    v.tensor_tensor_scan(hl[:, t, 0:CW], lru_a[:, 0:CW], lru_u[:, 0:CW], 0.0, ALU.mult, ALU.add)
                    dve.drain()
                    copy(lru_last[:, t, 0:1], hl[:, t, SEQ - 1:SEQ])
                    copy(lru_last[:, t, 1:9].unsqueeze(2), samples(hl[:, t, :], 3, 1)).then_inc(lru_free.sem, 1)

                def gla_cum(_=None):
                    dve.wait_ge(gla_ge.sem, gla_ge.at(layer, 1))
                    stt(tz[:, 0, :], tz[:, 0, :], 0.0, tz[:, 1, :], ALU.min, ALU.subtract)
                    dve.drain()
                    for c, off, n in CH:
                        v.tensor_tensor_scan(gqkc[:, 2, off:off + n], cst("reset_s") if c == SAMPLE else cst("ones").to_broadcast([P, n]),
                                             tz[:, 0, off:off + n], 0.0, ALU.mult, ALU.add)
                    dve.drain()

                def gla_pre_(c):
                    _, off, n = CH[c]
                    q, k, cum = (gqkc[:, i, off:off + n] for i in range(3))
                    if c < SAMPLE:
                        blocks = cum.rearrange("p (j i) -> p j i", j=4)
                        ref = blocks[:, :, 15:16]
                        tt(D[:], cum.unsqueeze(1).to_broadcast([P, 4, P]), ref.to_broadcast([P, 4, P]), ALU.subtract)
                        tt(ge[:, 0, :].rearrange("p (j i) -> p j i", j=4), ref.to_broadcast([P, 4, 32]), blocks, ALU.subtract)
                        tt(ge[:, 1, :], cum[:, n - 1:n].to_broadcast([P, n]), cum, ALU.subtract)
                        dve.drain()
                        ts(D[:], D[:], CLAMP, None, ALU.min)
                    else:
                        ts(ge[:, 0, 0:n], cum, -1.0, None, ALU.mult)
                        tt(by_sequence(ge[:, 1, 0:n]), by_sequence(cum)[:, :, SLEN - 1:SLEN].to_broadcast([P, NSEQ, SLEN]),
                           by_sequence(cum), ALU.subtract)
                        dve.drain()
                    ts(ge[:, 0, 0:n], ge[:, 0, 0:n], CLAMP, None, ALU.min)
                    copy(ge[:, 2, 0:n], cum)
                    dve.drain().then_inc(gla_diff.sem, 1)
                    dve.wait_ge(gla_exp.sem, gla_exp.at(layer, c + 1))
                    tt(ge[:, 0, 0:n], ge[:, 0, 0:n], k, ALU.mult)
                    if c < SAMPLE:
                        tt(D[:], D[:], q.unsqueeze(1).to_broadcast([P, 4, P]), ALU.mult)
                    tt(ge[:, 1, 0:n], ge[:, 1, 0:n], k, ALU.mult)
                    tt(qt[:, (c + 1) % 2, 0, 0:n], ge[:, 2, 0:n], q, ALU.mult)
                    dve.drain()
                    tt(kz[:, :, 0:n], ge[:, 0, 0:n].unsqueeze(1).to_broadcast([P, 4, n]),
                       per_head(cst("gla_heads"), P, n), ALU.mult)
                    dve.drain().then_inc(gla_pre.sem, 1)

                def gla_a_(c):
                    _, off, n = CH[c]
                    dve.wait_ge(gla_a.sem, gla_a.at(layer, c + 1))
                    tt(PT[0:n, :, 0:n], M[0][0:n, :].rearrange("p (h i) -> p h i", h=4)[:, :, 0:n],
                       masks(c, "keep").unsqueeze(1).to_broadcast([n, 4, n]), ALU.mult)
                    copy(V[0:n, :], M[1][0:n, 0:256])
                    copy(K[0:n, 0:P], M[1][0:n, 256:384])
                    dve.drain()
                    if c == SAMPLE:
                        dve.wait_ge(stored, layer * STORES + 64)
                        by_seq_values(V)
                        dve.drain()
                    dve.drain().then_inc(gla_bin.sem, 1)
                    if c < SAMPLE:
                        gla_pre_(c + 1)

                def gla_b_(c):
                    dve.wait_ge(gla_b.sem, gla_b.at(layer, c + 1))
                    if c == SAMPLE:
                        dve.wait_ge(s0_loaded.sem, s0_loaded.at(layer, 32))
                        s1 = S1[:, 0:512]
                        tt(s1.rearrange("p (b d) -> p b d", b=NSEQ), S0[:, 0:512].rearrange("p (b d) -> p b d", b=NSEQ),
                           gla_last[:, c % 2, :].unsqueeze(2).to_broadcast([P, NSEQ, 64]), ALU.mult)
                        dve.drain()
                        tt(s1, s1, M[0][:], ALU.add)
                    else:
                        tt((S_gla if c == 0 else dS)[:], M[3][:, 0:256], cst("gla_blocks"), ALU.mult)
                        if c:
                            dve.drain()
                            stt(S_gla[:], S_gla[:], gla_last[:, c % 2, 0:1], dS[:], ALU.mult, ALU.add)
                    dve.drain().then_inc(gla_s.sem, 1)

                def rotate(i):
                    buf, swapped = (rq, sq) if i else (rk[:], rv[:])
                    dve.wait_ge(rot_sent.sem, rot_sent.at(layer, 64 * (i + 1)))
                    for t in range(2):
                        tt(swapped[:, t, :], swapped[:, t, :], cst("sin"), ALU.mult)
                        tt(buf[:, t, :], buf[:, t, :], cst("cos"), ALU.mult)
                    dve.drain()
                    tt(buf[:], buf[:], swapped[:], ALU.add)
                    dve.drain().then_inc(rot_out.sem, 1)

                def ret_a_(c):
                    _, off, n = CH[c]
                    dve.wait_ge(ret_a.sem, ret_a.at(layer, c + 1))
                    decay = masks(c, "ret_decay").rearrange("p (t e i) -> p t e i", t=2, e=2)
                    scores = PT[0:n, :, 0:n].rearrange("p (t e) i -> p t e i", e=2)
                    for e in range(2):
                        tt(scores[:, :, e, :], M[e][0:n, 0:256].rearrange("p (t i) -> p t i", t=2)[:, :, 0:n],
                           decay[:, :, e, :], ALU.mult)
                    tt(heads(K[0:n, :]), heads(M[2][0:n, 0:256]), per_head(masks(c, "ret_k"), n, 64), ALU.mult)
                    copy(V[0:n, :], M[2][0:n, 256:512])
                    tt(qt[:, c % 2, :, 0:n], rq[:, :, off:off + n],
                       cst("ret_q_s" if c == SAMPLE else "ret_q").rearrange("p (t i) -> p t i", t=2), ALU.mult)
                    if c == SAMPLE:
                        dve.drain()
                        dve.wait_ge(stored, layer * STORES + 96)
                        by_seq_values(V)
                    dve.drain().then_inc(ret_bin.sem, 1)

                def ret_b_(c):
                    _, off, n = CH[c]
                    dve.wait_ge(ret_b.sem, ret_b.at(layer, c + 1))
                    if c == SAMPLE:
                        for e in range(2):
                            rows = slice(64 * e, 64 * e + 64)
                            copy(rv[rows, :, off:off + n], M[3 - e][rows, 0:2 * n].rearrange("p (t i) -> p t i", t=2))
                        dve.wait_ge(s0_loaded.sem, s0_loaded.at(layer, 48))
                        for t in range(2):
                            cols = slice(512 * t, 512 * t + 512)
                            stt(S1[:, cols], S0[:, cols], cst("ret_last_s")[:, t:t + 1], M[t][:], ALU.mult, ALU.add)
                    else:
                        copy(rv[:, :, off:off + n], M[3][:, 0:256].rearrange("p (t i) -> p t i", t=2))
                        tt((S_ret if c == 0 else dS)[:].rearrange("p (t d) -> p t d", t=2),
                           M[0][:, 0:256].rearrange("p (t d) -> p t d", t=2),
                           cst("ret_blocks").unsqueeze(1).to_broadcast([P, 2, P]), ALU.mult)
                        if c:
                            dve.drain()
                            for t in range(2):
                                cols = slice(P * t, P * t + P)
                                stt(S_ret[:, cols], S_ret[:, cols], cst("ret_last")[:, t:t + 1], dS[:, cols],
                                    ALU.mult, ALU.add)
                    dve.drain().then_inc(ret_s.sem, 1)

                def z_gate(t):
                    dve.wait_ge(gate_act.sem, gate_act.at(layer, t + 1))
                    tt(xbc[:, t, :], xbc[:, t, :], tz[:, t, :], ALU.mult)
                    if t:
                        dve.drain().then_inc(n_in.sem, 1)

                def norm_rstd(i, each, width):
                    dve.wait_ge(n_mm.sem, n_mm.at(layer, i + 1))
                    ts(rstd[:, 0:4 * each], M[4][:, 0:4 * each], 1.0 / width, EPS, ALU.mult, ALU.add)
                    ts(rstd[0:NS, 4 * each:5 * each], M[4][0:NS, 4 * each:5 * each], 1.0 / width, EPS,
                       ALU.mult, ALU.add).then_inc(n_mean.sem, 1)
                    dve.wait_ge(n_root.sem, n_root.at(layer, i + 1))
                    ins = v.reciprocal(rstd[:, 0:5 * each], rstd[:, 0:5 * each])
                    if each == 1:
                        ins = split_rstd()
                    ins.then_inc(n_rstd.sem, 1)

                def normed(buf, cols, gain, spread):
                    return stt(buf[:, cols], buf[:, cols], gain, spread, ALU.mult, ALU.mult)

                def low(i, g, t, src):
                    dve.wait_ge(y_hi.sem, y_hi.at(layer, i + 1))
                    tt(gl[g][:, t, :], src, gh[g][:, t, :].bitcast(F32), ALU.subtract).then_inc(y_lo.sem, 1)

                prompt, sample = slice(0, SEQ), slice(SEQ, TOK)

                def gla_norm_(i):
                    dve.wait_ge(n_spread.sem, n_spread.at(layer, i + 1))
                    if i < 2:
                        ins = normed(gv[:, i, :], prompt, par("gla_norm", i), M[4][:])
                    else:
                        for t in range(2):
                            ins = normed(gv[:, t, :], sample, par("gla_norm", t), M[4][:, t * NS:(t + 1) * NS])
                    ins.then_inc(n_used.sem, 1)

                def ssd_norm_(i):
                    dve.wait_ge(n_spread.sem, n_spread.at(layer, 4 + i))
                    for t in range(2):
                        ins = normed(xbc[:, t, :], sample if i else prompt, par("ssd_norm", t),
                                     M[4][:, 0:NS] if i else M[4][:])
                    ins.then_inc(n_used.sem, 1)
                    if i:
                        dve.drain().then_inc(y_out.sem, 2)
                        low(0, G_SSD, 0, xbc[:, 0, :])
                        low(1, G_SSD, 1, xbc[:, 1, :])

                def gla_out(t):
                    dve.wait_ge(gate_act.sem, gate_act.at(layer, 5 + t))
                    tt(tz[:, t, :], tz[:, t, :], gv[:, t, :], ALU.mult).then_inc(y_out.sem, 1)
                    low(4 + t, G_GLA, t, tz[:, t, :])

                def lru_out(t):
                    dve.wait_ge(gate_act.sem, gate_act.at(layer, 3 + t))
                    tt(tz[:, t, prompt], tz[:, t, prompt], hl[:, t, prompt], ALU.mult)
                    tt(by_sequence(tz[:, t, sample]), by_sequence(tz[:, t, sample]), samples(hl[:, t, :], 0),
                       ALU.mult).then_inc(y_out.sem, 1)
                    low(2 + t, G_LRU, t, tz[:, t, :])

                def centre(_=None):
                    dve.wait_ge(cent_mm.sem, cent_mm.at(layer, 1))
                    for t in range(2):
                        copy(rv[:, t, prompt], M[t][:])
                        copy(rv[:, t, sample], M[2][:, t * NS:(t + 1) * NS])
                    dve.drain().then_inc(cent_out.sem, 1)

                def ret_norm_(_=None):
                    dve.wait_ge(n_spread.sem, n_spread.at(layer, 6))
                    for t in range(2):
                        normed(rv[:, t, :], prompt, par("ret_norm", t), M[t][:])
                        ins = normed(rv[:, t, :], sample, par("ret_norm", t), M[2][:, t * NS:(t + 1) * NS])
                    ins.then_inc(n_used.sem, 1)
                    dve.drain()

                def ret_out(t):
                    dve.wait_ge(gate_act.sem, gate_act.at(layer, 7 + t))
                    tt(rv[:, t, :], rv[:, t, :], ret_gate[:, t, :], ALU.mult).then_inc(y_out.sem, 1)
                    low(6 + t, G_RET, t, rv[:, t, :])

                stages = {
                    "dt": dt, "ssd_a": ssd_a_, "ssd_b": ssd_b_, "lru_scan": lru_scan, "gla_cum": gla_cum,
                    "gla_pre": gla_pre_, "gla_a": gla_a_, "gla_b": gla_b_, "rotate": rotate, "ret_a": ret_a_,
                    "ret_b": ret_b_, "ret_out": ret_out, "z_gate": z_gate, "gla_stat": lambda: norm_rstd(0, 4, 64), "gla_norm": gla_norm_,
                    "ssd_stat": lambda: norm_rstd(1, 1, 256), "ssd_norm": ssd_norm_, "gla_out": gla_out,
                    "lru_out": lru_out, "centre": centre, "ret_stat": lambda: norm_rstd(2, 4, 64),
                    "ret_norm": ret_norm_,
                }
                for s in range(2 * NIN):
                    evacuate(s // 2, s % 2)
                    for name, *args in SLOTS.get(s, []):
                        if name in stages:
                            stages[name](*args)

                def add_to_h(u, m):
                    for half in range(2):
                        acc, cols = take(u, half)
                        ins = tt(h[:, m, cols], h[:, m, cols], acc, ALU.add)
                        ins.then_inc(dense_free.sem, 1 + (2 * PAD if (u, half) == (NUNIT - 1, 1) else 0))

                def new_h(i, u0, gain):
                    for m in range(KT):
                        add_to_h(u0 + m, m)
                        dve.drain().then_inc(h_new.sem, 1)
                        if m:
                            xl_tile(layer, i, m - 1, par(gain, m - 1))
                    xl_tile(layer, i, KT - 1, par(gain, KT - 1))
                    rms_rstd(layer, i)

                new_h(0, OUT0, "norm_ffn")

                def ffn_pair(j, count, taken):
                    dve.drain()
                    for i in range(4):
                        acc, cols = taken(i)
                        tt(tz[:, i // 2, cols], acc, rs_bcast[:, cols], ALU.mult).then_inc(dense_free.sem, 1)
                        if i == 1:
                            dve.drain().then_inc(gate_out.sem, 1)
                    dve.drain()
                    dve.wait_ge(gate_silu.sem, count)
                    tt(tz[:, 1, :], tz[:, 1, :], tz[:, 0, :], ALU.mult).then_inc(act_out.sem, 1)
                    dve.wait_ge(act_hi.sem, count)
                    hi, lo = operand(j)
                    tt(lo, tz[:, 1, :], hi.bitcast(F32), ALU.subtract).then_inc(act_lo.sem, 1)

                with dve.Fori(0, NGRP) as g:
                    def take_g(i, half):
                        q = 2 * (FFN0 + i) + half
                        dve.wait_ge(dense_done, layer * (2 * LU) + g * (2 * GU) + (q + 1))
                        return dense[q % 3][:, 0:HALF], slice(half * HALF, (half + 1) * HALF)

                    for j in range(GROUP):
                        ffn_pair(j, layer * FT + g * GROUP + (j + 1), lambda i: take_g(2 * j + i // 2, i % 2))
                    for m in range(KT):
                        for half in range(2):
                            acc, cols = take_g(2 * GROUP + m, half)
                            tt(h[:, m, cols], h[:, m, cols], acc, ALU.add).then_inc(dense_free.sem, 1)
                for j in range(REST):
                    ffn_pair(j, layer * FT + (NGRP * GROUP + j + 1), lambda i: take(REST0 + 2 * j + i // 2, i % 2))
                new_h(1, REST0 + 2 * REST, "norm_next")
                dve.drain().then_inc(params_free.sem, 1)

            for m in range(KT):
                stt(h[:, m, :], h[:, m, :], par("norm_next", m), rs_bcast[:], ALU.mult, ALU.mult).then_inc(y_final, 1)

        @block.tensor
        def _(pe):
            mm = nc.tensor.matmul

            def turn(out, src, n_in=P):
                return mm(out, src, exact("ident", n_in, 0, n_in).bitcast(F32), start=True, stop=True)

            def spread(out, c):
                n = CH[c][2]
                mm(out, rstd_hi[0:n, c:c + 1].to_broadcast([n, P]), exact("ident", n, 0, n), start=True, stop=False)
                return mm(out, rstd_lo[0:n, c:c + 1].to_broadcast([n, P]), exact("ident", n, 0, n),
                          start=False, stop=True)

            def square_sums(layer, i):
                pe.wait_ge(sq_added.sem, sq_added.at(layer, (i + 1) * (KT - 1)))
                for c, off, n in CH:
                    ins = mm(M[4][0:n, c:c + 1], sq_sum[:, off:off + n], cst("ones"), start=True, stop=True)
                ins.then_inc(stat_done.sem, 1)

            def spread_rstd(layer, i):
                pe.wait_ge(rstd_done.sem, rstd_done.at(layer, i + 1))
                for c, off, n in CH:
                    ins = spread(M[1][:, 0:n] if c == SAMPLE else M[0][:, off:off + n], c)
                ins.then_inc(rs_spread.sem, 1)

            with pe.Fori(0, DEPTH) as layer:

                def half_unit(first, q, slot, n_unit, rhs, ks, before=None, inc=1, steps=None):
                    steps = range(len(ks)) if steps is None else steps
                    if steps[0] == 0:
                        pe.wait_ge(dense_free.sem, first)
                        if q % 2 == 0:
                            pe.wait_ge(lo_done, n_unit)
                    cols = slice(q % 2 * HALF, (q % 2 + 1) * HALF)
                    bank_ = dense[q % 3][:, 0:HALF]
                    for i in steps:
                        if before is not None and q % 2 == 0:
                            before(i)
                        hi, lo = rhs(ks[i])
                        w = slice(i * P, (i + 1) * P)
                        for j, (wt, xx) in enumerate(((wh, hi), (wh, lo), (wl, hi))):
                            ins = mm(bank_, wt[:, slot, w], xx[:, cols], start=(i == 0 and j == 0),
                                     stop=(i == len(ks) - 1 and j == 2))
                    if steps[-1] == len(ks) - 1:
                        ins.then_inc(dense_done, inc)

                def unit_half(u, half, rhs, ks, before=None, steps=None):
                    q = 2 * u + half
                    half_unit(layer * (2 * LU) + (q + 1), q, u % RING, layer * LU + (u + 1), rhs, ks, before,
                              1 + (2 * PAD if (u, half) == (NUNIT - 1, 1) else 0), steps)

                def x_operand(k):
                    return xh[:, k, :], xl[:, k, :]

                def dt(_=None):
                    pe.wait_ge(dt_out.sem, dt_out.at(layer, 1))
                    for c, off, n in CH:
                        ins = mm(M[4][0:n, 4 * c:4 * c + 4], misc[32:36, off:off + n], cx[32:36, 32:36].bitcast(F32),
                                 start=True, stop=True)
                    ins.then_inc(dt_turned.sem, 1)

                def ssd_a_(c):
                    _, off, n = CH[c]
                    if c == 0:
                        pe.wait_ge(dt_ready.sem, dt_ready.at(layer, 1))
                        pe.wait_ge(conv_silu.sem, conv_silu.at(layer, 4))
                    else:
                        pe.wait_ge(ssd_s.sem, ssd_s.at(layer, c))
                    s_ = "_s" if c == SAMPLE else ""
                    w = NS + NSEQ if c == SAMPLE else P
                    parts = (log_a_hi, log_a_lo)
                    for r in range(2):
                        for g in range(2):
                            mm(M[1][64 * g:64 * g + 64, r * P:r * P + w],
                               log_a[0:n, c, 2 * g + r:2 * g + r + 1].to_broadcast([n, 64]),
                               exact("upper" + s_, n).bitcast(F32), start=True, stop=True)
                    mm(M[1][0:n, 256:260], masks(c, "after"), log_a[0:n, c, :], start=True, stop=True)
                    rows4 = M[0][0:n, :].rearrange("p (h i) -> p h i", h=4)[:, :, 0:n]
                    mm(rows4, exact("ident", n, 0, n), exact("neg" + s_, n).unsqueeze(1).to_broadcast([n, 4, n]),
                       start=True, stop=False, skip_group_check=True)
                    for part in parts:
                        mm(rows4, exact("minus" + s_, n), part[0:n, c, :].unsqueeze(2).to_broadcast([n, 4, n]),
                           start=False, stop=False, skip_group_check=True)
                    for hd in range(4):
                        for part in parts:
                            mm(M[0][0:n, hd * P:hd * P + n], part[0:n, c, hd:hd + 1].to_broadcast([n, n]),
                               exact("upper" + s_, n, 0, n), start=False, stop=part is log_a_lo, skip_group_check=True)
                    for g in range(2):
                        rows = slice(64 * g, 64 * g + 64)
                        mm(M[2 + g][0:n, 0:n], xbc[rows, 2, off:off + n], xbc[rows, 3, off:off + n], start=True, stop=True)
                    for t in range(3):
                        ins = turn(M[2][0:n, P * (t + 1):P * (t + 2)], xbc[:, t, off:off + n])
                    ins.then_inc(ssd_a.sem, 1)

                def ssd_b_(c):
                    _, off, n = CH[c]
                    pe.wait_ge(ssd_bin.sem, ssd_bin.at(layer, c + 1))
                    if c == SAMPLE:
                        pe.wait_ge(s0_loaded.sem, s0_loaded.at(layer, 16))
                    for hd in range(4):
                        g, r = hd // 2, hd % 2
                        out = M[g][64 * r:64 * r + 64, 0:n]
                        v = V[0:n, 64 * hd:64 * hd + 64]
                        mm(out, v, PT[0:n, hd, 0:n], start=True, stop=c in (0, SAMPLE), skip_group_check=c == SAMPLE)
                        if 0 < c < SAMPLE:
                            mm(out, S_ssd[:, 64 * hd:64 * hd + 64], qt[:, c % 2, r, 0:n], start=False, stop=True)
                    if c < SAMPLE:
                        mm(M[2][:, 0:256], K[0:n, 0:P], Vd[0:n, :], start=True, stop=True).then_inc(ssd_b.sem, 1)
                        return
                    for r in range(2):
                        for g in range(2):
                            rows = slice(64 * g, 64 * g + 64)
                            for b in range(NSEQ):
                                at = (r * NSEQ + b) * 64
                                mm(M[g][64 * r:64 * r + 64, SLEN * b:SLEN * (b + 1)], S0[rows, at:at + 64],
                                   qt[rows, c % 2, r, SLEN * b:SLEN * (b + 1)], start=False, stop=True,
                                   skip_group_check=True)
                    for hd in range(4):
                        g, r = hd // 2, hd % 2
                        ins = mm(M[2 + r][64 * g:64 * g + 64, :], K[0:n, 64 * g:64 * g + 64],
                                 Vx[0:n, 512 * hd:512 * hd + 512], start=True, stop=True)
                    ins.then_inc(ssd_b.sem, 1)

                def lru_gates(t):
                    if t == 0:
                        pe.wait_ge(conv_done.sem, conv_done.at(layer, 6))
                        pe.wait_ge(ssd_s.sem, ssd_s.at(layer, 5))
                    else:
                        pe.wait_ge(lru_sig.sem, lru_sig.at(layer, 1))
                    w = par("lru_w", 0, 512)
                    for i in range(2):
                        for b in range(2):
                            ins = mm(M[2 * i + b][:, 0:CW // 2], w[:, (2 * i + t) * P:(2 * i + t + 1) * P],
                                     lru_x[:, t, b * (CW // 2):(b + 1) * (CW // 2)], start=True, stop=True)
                    ins.then_inc(lru_mm.sem, 1)

                def gla_gate(_=None):
                    pe.wait_ge(params_loaded.sem, params_loaded.at(layer, 16))
                    for b in range(2):
                        ins = mm(M[b][:, 0:HALF], par("gate2", 0, P)[0:16], misc[0:16, b * HALF:(b + 1) * HALF],
                                 start=True, stop=True)
                    ins.then_inc(gla_gmm.sem, 1)

                def gla_a_(c):
                    _, off, n = CH[c]
                    pe.wait_ge(gla_pre.sem, gla_pre.at(layer, c + 1))
                    if c == 0:
                        pe.wait_ge(lru_sig.sem, lru_sig.at(layer, 2))
                    if c < SAMPLE:
                        for j in range(4):
                            for hd in range(4):
                                mm(M[0][32 * j:32 * j + 32, hd * P:(hd + 1) * P], kz[:, hd, 32 * j:32 * j + 32],
                                   D[:, j, :], start=True, stop=True)
                    else:
                        for hd in range(4):
                            mm(M[0][0:n, hd * P:hd * P + n], kz[:, hd, 0:n], qt[:, (c + 1) % 2, 0, 0:n], start=True, stop=True)
                    for t in range(2):
                        turn(M[1][0:n, t * P:(t + 1) * P], gv[:, t, off:off + n])
                    turn(M[1][0:n, 256:384], ge[:, 1, 0:n]).then_inc(gla_a.sem, 1)

                def gla_b_(c):
                    _, off, n = CH[c]
                    pe.wait_ge(gla_bin.sem, gla_bin.at(layer, c + 1))
                    if c:
                        pe.wait_ge(gla_s.sem, gla_s.at(layer, c))
                        pe.wait_ge(gla_o.sem, gla_o.at(layer, c))
                    if c == SAMPLE:
                        pe.wait_ge(s0_loaded.sem, s0_loaded.at(layer, 32))
                    for hd in range(4):
                        t, e = hd // 2, hd % 2
                        out = (M[2 + t] if c == SAMPLE else M[2])[64 * e:64 * e + 64]
                        out = out[:, 0:n] if c == SAMPLE else out[:, t * P:t * P + n]
                        mm(out, V[0:n, 64 * hd:64 * hd + 64], PT[0:n, hd, 0:n], start=True, stop=c in (0, SAMPLE),
                           skip_group_check=c > 0)
                        if e and 0 < c < SAMPLE:
                            mm(M[2][:, t * P:t * P + n], S_gla[:, t * P:(t + 1) * P], qt[:, (c + 1) % 2, 0, 0:n],
                               start=False, stop=True, skip_group_check=True)
                    if c < SAMPLE:
                        mm(M[3][:, 0:256], K[0:n, 0:P], V[0:n, :], start=True, stop=True).then_inc(gla_b.sem, 1)
                        return
                    pe.drain()
                    for hd in (0, 2, 1, 3):
                        t, e = hd // 2, hd % 2
                        rows = slice(32 * hd, 32 * hd + 32)
                        for b in range(NSEQ):
                            cols = slice(SLEN * b, SLEN * (b + 1))
                            mm(M[2 + t][64 * e:64 * e + 64, cols], S0[rows, 64 * b:64 * b + 64], qt[rows, (c + 1) % 2, 0, cols],
                               start=False, stop=True, skip_group_check=True, tile_position=(32 * hd, 64 * e))
                    for hd in range(4):
                        ins = mm(M[0][32 * hd:32 * hd + 32, :], K[0:n, 32 * hd:32 * hd + 32],
                                 Vx[0:n, 512 * hd:512 * hd + 512], start=True, stop=True, tile_position=(0, 32 * hd))
                    ins.then_inc(gla_b.sem, 1)

                def ret_a_(c):
                    _, off, n = CH[c]
                    if c == 0:
                        pe.wait_ge(rot_out.sem, rot_out.at(layer, 2))
                        pe.wait_ge(gla_s.sem, gla_s.at(layer, 5))
                        pe.wait_ge(gla_o.sem, gla_o.at(layer, 5))
                    else:
                        pe.wait_ge(ret_s.sem, ret_s.at(layer, c))
                    for t in range(2):
                        turn(M[2][0:n, t * P:(t + 1) * P], rk[:, t, off:off + n])
                    for t in range(2):
                        for e in range(2):
                            rows = slice(64 * e, 64 * e + 64)
                            mm(M[e][0:n, t * P:t * P + n], rk[rows, t, off:off + n], rq[rows, t, off:off + n],
                               start=True, stop=True)
                    for t in range(2):
                        ins = turn(M[2][0:n, 256 + t * P:256 + (t + 1) * P], rv[:, t, off:off + n])
                    ins.then_inc(ret_a.sem, 1)

                def ret_b_(c):
                    _, off, n = CH[c]
                    pe.wait_ge(ret_bin.sem, ret_bin.at(layer, c + 1))
                    if c == SAMPLE:
                        pe.wait_ge(s0_loaded.sem, s0_loaded.at(layer, 48))
                    for hd in range(4):
                        t, e = hd // 2, hd % 2
                        out = M[3 - e][64 * e:64 * e + 64, t * n:(t + 1) * n] if c == SAMPLE else \
                            M[3][64 * e:64 * e + 64, t * P:t * P + n]
                        mm(out, V[0:n, 64 * hd:64 * hd + 64], PT[0:n, hd, 0:n], start=True, stop=c in (0, SAMPLE),
                           skip_group_check=c > 0)
                        if e and 0 < c < SAMPLE:
                            mm(M[3][:, t * P:t * P + n], S_ret[:, t * P:(t + 1) * P], qt[:, c % 2, t, 0:n],
                               start=False, stop=True, skip_group_check=True)
                        if c == SAMPLE:
                            rows = slice(64 * e, 64 * e + 64)
                            for b in range(NSEQ):
                                at = (t * NSEQ + b) * 64
                                mm(out[:, SLEN * b:SLEN * (b + 1)], S0[rows, at:at + 64],
                                   qt[rows, c % 2, t, SLEN * b:SLEN * (b + 1)], start=False, stop=True,
                                   skip_group_check=True)
                    if c < SAMPLE:
                        for t in range(2):
                            ins = mm(M[0][:, t * P:(t + 1) * P], K[0:n, t * P:(t + 1) * P], V[0:n, t * P:(t + 1) * P],
                                     start=True, stop=True)
                    else:
                        for hd in range(4):
                            t, e = hd // 2, hd % 2
                            ins = mm(M[t][64 * e:64 * e + 64, :], K[0:n, 64 * hd:64 * hd + 64],
                                     Vx[0:n, 512 * hd:512 * hd + 512], start=True, stop=True)
                    ins.then_inc(ret_b.sem, 1)

                def head_stat(i):
                    pe.wait_ge(n_sq.sem, n_sq.at(layer, i + 1))
                    if i:
                        pe.wait_ge(n_used.sem, n_used.at(layer, 5))
                    for c, off, n in CH:
                        for t in range(2):
                            at = 4 * c + 2 * t
                            ins = mm(M[4][0:n, at:at + 2], sq[:, t, off:off + n], cst("pair"), start=True, stop=True)
                    ins.then_inc(n_mm.sem, 1)

                def head_spread(out, c, t):
                    n = CH[c][2]
                    for e in range(2):
                        ins = mm(out[64 * e:64 * e + 64],
                                 rstd[0:n, 4 * c + 2 * t + e:4 * c + 2 * t + e + 1].to_broadcast([n, 64]),
                                 exact("ident", n, 0, n).bitcast(F32), start=True, stop=True)
                    return ins

                def gla_norm_(i):
                    if i == 0:
                        pe.wait_ge(n_rstd.sem, n_rstd.at(layer, 1))
                    else:
                        pe.wait_ge(n_used.sem, n_used.at(layer, i))
                    if i < 2:
                        for c in range(4):
                            ins = head_spread(M[4][:, c * P:(c + 1) * P], c, i)
                    else:
                        for t in range(2):
                            ins = head_spread(M[4][:, t * NS:(t + 1) * NS], SAMPLE, t)
                    ins.then_inc(n_spread.sem, 1)

                def ssd_stat(_=None):
                    pe.wait_ge(n_sq.sem, n_sq.at(layer, 2))
                    pe.wait_ge(n_used.sem, n_used.at(layer, 3))
                    for c, off, n in CH:
                        for t in range(2):
                            ins = mm(M[4][0:n, c:c + 1], sq[:, t, off:off + n], cst("ones", P, 0, 1),
                                     start=(t == 0), stop=(t == 1))
                    ins.then_inc(n_mm.sem, 1)

                def ssd_norm_(i):
                    if i == 0:
                        pe.wait_ge(n_rstd.sem, n_rstd.at(layer, 2))
                    else:
                        pe.wait_ge(n_used.sem, n_used.at(layer, 4))
                    for c in ([SAMPLE] if i else range(4)):
                        n = CH[c][2]
                        out = M[4][:, 0:n] if i else M[4][:, c * P:(c + 1) * P]
                        ins = spread(out, c)
                    ins.then_inc(n_spread.sem, 1)

                def centre(_=None):
                    pe.wait_ge(ret_s.sem, ret_s.at(layer, 5))
                    for t in range(2):
                        mm(M[t][:], cst("centre"), rv[:, t, 0:SEQ], start=True, stop=True)
                        ins = mm(M[2][:, t * NS:(t + 1) * NS], cst("centre"), rv[:, t, SEQ:TOK], start=True, stop=True)
                    ins.then_inc(cent_mm.sem, 1)

                def ret_norm_(_=None):
                    pe.wait_ge(n_rstd.sem, n_rstd.at(layer, 3))
                    for t in range(2):
                        for c in range(4):
                            head_spread(M[t][:, c * P:(c + 1) * P], c, t)
                        ins = head_spread(M[2][:, t * NS:(t + 1) * NS], SAMPLE, t)
                    ins.then_inc(n_spread.sem, 1)

                stages = {
                    "dt": dt, "ssd_a": ssd_a_, "ssd_b": ssd_b_, "lru_gates": lru_gates, "gla_gate": gla_gate,
                    "gla_a": gla_a_, "gla_b": gla_b_, "ret_a": ret_a_, "ret_b": ret_b_,
                    "gla_stat": lambda: head_stat(0), "gla_norm": gla_norm_, "ssd_stat": ssd_stat,
                    "ssd_norm": ssd_norm_, "centre": centre, "ret_stat": lambda: head_stat(2), "ret_norm": ret_norm_,
                }
                for s in range(2 * NIN):
                    def operand_ready(k, s=s):
                        if s == 0:
                            pe.wait_ge(xl_done.sem, xl_done.at(layer, k + 1 - KT))
                    unit_half(s // 2, s % 2, x_operand, range(KT), operand_ready)
                    if s == 0:
                        pe.wait_ge(consts_loaded, 16)
                        pe.wait_ge(exact_done, 1)
                        square_sums(layer, -1)
                    if s == 1:
                        spread_rstd(layer, -1)
                    for name, *args in SLOTS.get(s, []):
                        if name in stages:
                            stages[name](*args)

                def result_ready(i):
                    pe.wait_ge(y_lo.sem, y_lo.at(layer, i + 1))
                for steps in (range(KT - 2), range(KT - 2, KT)):
                    for half in range(2):
                        unit_half(OUT0, half, operand, OUT_K, result_ready, steps)
                for m in range(1, KT):
                    for half in range(2):
                        unit_half(OUT0 + m, half, operand, OUT_K)

                def norm_ready(k):
                    pe.wait_ge(xl_done.sem, xl_done.at(layer, k + 1))
                unit_half(FFN0, 0, x_operand, range(KT), norm_ready)
                square_sums(layer, 0)
                unit_half(FFN0, 1, x_operand, range(KT))
                spread_rstd(layer, 0)

                with pe.Fori(0, NGRP) as g:
                    for i in range(1, GU + 1):
                        def ready(k, i=i):
                            if i == 2 * GROUP:
                                pe.wait_ge(act_lo.sem, layer * FT + g * GROUP + (k + 1))
                        for half in range(2):
                            q = 2 * (FFN0 + i) + half
                            half_unit(layer * (2 * LU) + g * (2 * GU) + (q + 1), q, i % RING,
                                      layer * LU + g * GU + (FFN0 + i + 1),
                                      operand if 2 * GROUP <= i < GU else x_operand, range(KT), ready)
                for i in range(1, 2 * REST + KT):
                    def ready(k, i=i):
                        if i == 2 * REST:
                            pe.wait_ge(act_lo.sem, act_lo.at(layer, NGRP * GROUP + k + 1))
                    for half in range(2):
                        if i < 2 * REST:
                            unit_half(REST0 + i, half, x_operand, range(KT), ready)
                        else:
                            unit_half(REST0 + i, half, operand, range(REST), ready)

            square_sums(DEPTH, -1)
            spread_rstd(DEPTH, -1)



def cut(a):
    a = np.asarray(a)
    return np.moveaxis(a.reshape(a.shape[0] // P, P, *a.shape[1:]), 0, 1)


def constants():
    out = np.zeros((P, NCONST + NEXACT), np.float32)

    def put(name, a):
        a = np.asarray(a, np.float64)
        at, w = CONST[name] if name in CONST else EXACT[name]
        at += 0 if name in CONST else NCONST
        out[:a.shape[0], at:at + w] = a.reshape(a.shape[0], -1)

    p, q = np.arange(P)[:, None], np.arange(P)[None, :]
    masked = -2.0 ** 100
    put("ident", p == q)
    put("upper", p <= q)
    put("minus", np.where(p <= q, -1.0, 0.0))
    put("neg", np.where(p <= q, 0.0, masked))
    put("after", p > q)
    put("keep", p <= q)
    put("centre", (p == q) - (p // 64 == q // 64) / 64.0)
    put("ones", np.ones((P, 1)))
    wide = np.arange(256)[None, :]
    put("ssd_blocks", p // 64 == wide // 128)
    put("gla_blocks", p // 32 == wide // 64)
    put("ret_blocks", p // 64 == q // 64)
    log_gamma = np.log(1.0 - 2.0 ** (-5.0 - np.arange(4)))
    scale = 64 ** -0.5
    lg = log_gamma[None, :, None]
    put("ret_decay", np.where(p[:, None] <= q[None], scale * np.exp(lg * (q[None] - p[:, None])), 0.0))
    head = 2 * np.arange(2)[None, :] + p // 64
    put("ret_q", np.exp(log_gamma[head][:, :, None] * (np.arange(P) + 1)))
    put("ret_k", scale * np.exp(log_gamma[None] * (P - 1 - p)))
    put("ret_last", np.exp(log_gamma[head] * P))
    put("ret_last_s", np.exp(log_gamma[head] * SLEN))
    j, i = np.arange(NS)[:, None], np.arange(NS)[None, :]
    same = j // SLEN == i // SLEN
    seq = j // SLEN == np.arange(NSEQ)[None, :]
    put("upper_s", np.concatenate([same & (j <= i), seq], axis=1))
    put("minus_s", np.where(same & (j <= i), -1.0, 0.0))
    put("neg_s", np.where(same & (j <= i), 0.0, masked))
    put("after_s", same & (j > i))
    put("keep_s", same & (j <= i))
    put("seq_s", seq)
    put("reset_s", np.broadcast_to(i % SLEN != 0, (P, NS)))
    put("ret_decay_s", np.where((same & (j <= i))[:, None], scale * np.exp(lg * (i[None] - j[:, None])), 0.0))
    put("ret_q_s", np.exp(log_gamma[head][:, :, None] * (np.arange(NS) % SLEN + 1)))
    put("ret_k_s", scale * np.exp(log_gamma[None] * (SLEN - 1 - j % SLEN)))
    put("gla_heads", p // GDK == np.arange(4)[None, :])
    put("pair", p // 64 == np.arange(2)[None, :])
    inv = (10000.0 ** (-np.arange(32) / 32.0)).astype(np.float32)
    pos = np.concatenate([np.arange(SEQ), PAST + np.arange(NS) % SLEN]).astype(np.float32)
    ang = (pos[None, :] * inv[:, None]).astype(np.float32).astype(np.float64)
    put("cos", np.tile(np.cos(ang), (4, 1)))
    put("sin", np.tile(np.concatenate([-np.sin(ang), np.sin(ang)]), (2, 1)))
    return out


def pack_weights(w_in, w_out, w_gate, w_up, w_down):
    units = np.zeros((DEPTH * LU + RING, P, KT, P), np.float32)
    lr0, dt0 = 2308, 768
    for d in range(DEPTH):
        out = units[d * LU:(d + 1) * LU]
        for u, (_, c) in enumerate(IN_UNITS):
            if c is None:
                out[u, :, :, 0:16] = cut(w_in[d][:, lr0:lr0 + 16])
                out[u, :, :, 32:36] = cut(w_in[d][:, dt0:dt0 + 4])
            else:
                out[u] = cut(w_in[d][:, c:c + P])
        for m in range(KT):
            out[OUT0 + m] = cut(w_out[d][:, m * P:(m + 1) * P])[:, OUT_K]
        u = FFN0
        for first in range(0, FT, GROUP):
            n = min(GROUP, FT - first)
            for j in range(first, first + n):
                out[u] = cut(w_gate[d][:, j * P:(j + 1) * P])
                out[u + 1] = cut(w_up[d][:, j * P:(j + 1) * P])
                u += 2
            for m in range(KT):
                out[u, :, 0:n] = cut(w_down[d][first * P:(first + n) * P, m * P:(m + 1) * P])
                u += 1
    return units.reshape(DEPTH * LU + RING, P, KT * P)


def pack_params(i):
    out = np.zeros((DEPTH, P, NPARAM), np.float32)
    for d in range(DEPTH):
        def put(name, a):
            at, w = PARAM[name]
            out[d, :a.shape[0], at:at + w] = a.reshape(a.shape[0], -1)

        def taps(w):
            return np.moveaxis(cut(w.T), -1, 2)

        put("norm_ffn", cut(i["norm_ffn"][d]))
        put("norm_next", cut(i["norm_mix"][d + 1] if d + 1 < DEPTH else i["norm_final"]))
        put("ssd_conv_w", taps(i["ssd_conv_w"][d]))
        put("lru_conv_w", taps(i["lru_conv_w"][d]))
        for name in ("ssd_conv_b", "lru_conv_b", "ssd_norm", "ret_norm", "gla_norm", "lru_b_a", "lru_b_x", "lru_lambda"):
            put(name, cut(i[name][d]))
        put("gla_b", cut(i["gla_b_gate"][d]))
        put("ssd_d", cut(np.repeat(i["ssd_d"][d], 64)))
        put("dt_bias", np.broadcast_to(i["ssd_dt_bias"][d], (P, 4)))
        put("a_log", np.broadcast_to(i["ssd_a_log"][d], (P, 4)))
        put("lru_h0", cut(i["state_lru"][d].T))
        history = np.concatenate([i["state_ssd_conv"][d], i["state_lru_conv"][d]], axis=-1)
        put("history", cut(np.transpose(history, (2, 0, 1))))
        w = np.zeros((P, 2, 2, P), np.float32)
        for k, name in enumerate(("lru_w_a", "lru_w_x")):
            for b in range(4):
                r = slice(64 * (b % 2), 64 * (b % 2) + 64)
                w[r, k, b // 2, r] = i[name][d][b]
        put("lru_w", w)
        put("gate2", i["gla_w_gate2"][d])
    return out


def kernel(**inputs):
    import concourse.bacc as bacc
    from concourse.bass_utils import run_bass_kernel_spmd

    i = {k: np.asarray(v) for k, v in inputs.items()}
    x = np.concatenate([i["x_prompt"].reshape(SEQ, DM), i["x_sample"].reshape(NS, DM)]).T
    first_gain, table = cut(i["norm_mix"][0]), constants()
    arrays = {
        "weights": pack_weights(i["w_in"], i["w_out"], i["w_gate"], i["w_up"], i["w_down"]),
        "params": pack_params(i),
        "consts": np.concatenate([table[:, :NCONST], first_gain, table[:, NCONST:]], axis=1),
        "x": np.ascontiguousarray(cut(x)),
        "s_ssd": i["state_ssd"].reshape(DEPTH, NSEQ, 2, 2, 64, 64).transpose(0, 2, 4, 3, 1, 5).reshape(DEPTH, P, 1024),
        "s_ret": i["state_ret"].reshape(DEPTH, NSEQ, 2, 2, 64, 64).transpose(0, 3, 4, 2, 1, 5).reshape(DEPTH, P, 1024),
        "s_gla": i["state_gla"].transpose(0, 2, 3, 1, 4).reshape(DEPTH, P, 512),
    }
    outs = {"y": (P, KT, TOK), "o_conv": (DEPTH, P, 6, 27), "o_ssd": (DEPTH, P, 256), "o_ret": (DEPTH, P, 256),
            "o_gla": (DEPTH, P, 256), "o_lru": (DEPTH, P, 2, 9), "n_ssd": (DEPTH, P, 1024),
            "n_ret": (DEPTH, P, 1024), "n_gla": (DEPTH, P, 512)}
    nc = bacc.Bacc("TRN2", target_bir_lowering=False, num_devices=1)
    arrays = {k: np.ascontiguousarray(v) for k, v in arrays.items()}
    args = {k: nc.dram_tensor(k, v.shape, F32, kind="ExternalInput").ap() for k, v in arrays.items()}
    args |= {k: nc.dram_tensor(k, shape, F32, kind="ExternalOutput").ap() for k, shape in outs.items()}
    trunk(nc, **args)
    r = run_bass_kernel_spmd(nc, [arrays], core_ids=[0]).results[0]

    y = np.moveaxis(r["y"], 1, 0).reshape(DM, TOK).T
    conv = r["o_conv"].transpose(0, 3, 2, 1).reshape(DEPTH, 27, 6 * P)
    lru = r["o_lru"].transpose(0, 3, 2, 1).reshape(DEPTH, 9, 2 * P)
    conv_p, conv_s = conv[:, None, 0:3], conv[:, 3:].reshape(DEPTH, NSEQ, 3, 6 * P)
    o_ssd = r["o_ssd"].reshape(DEPTH, 2, 64, 2, 2, 64)
    o_ret = r["o_ret"].reshape(DEPTH, 2, 64, 2, 2, 64)
    o_gla = r["o_gla"].reshape(DEPTH, 4, 32, 4, 64)
    p_ssd = np.stack([o_ssd[:, h // 2, :, h // 2, h % 2] for h in range(4)], axis=1)[:, None]
    p_ret = np.stack([o_ret[:, h % 2, :, h // 2, h % 2] for h in range(4)], axis=1)[:, None]
    p_gla = np.stack([o_gla[:, h, :, h] for h in range(4)], axis=1)[:, None]
    s_ssd = r["n_ssd"].reshape(DEPTH, 2, 64, 2, NSEQ, 64).transpose(0, 4, 1, 3, 2, 5).reshape(DEPTH, NSEQ, 4, 64, 64)
    s_ret = r["n_ret"].reshape(DEPTH, 2, 64, 2, NSEQ, 64).transpose(0, 4, 3, 1, 2, 5).reshape(DEPTH, NSEQ, 4, 64, 64)
    s_gla = r["n_gla"].reshape(DEPTH, 4, 32, NSEQ, 64).transpose(0, 3, 1, 2, 4)
    out = (y[:SEQ].reshape(1, SEQ, DM), y[SEQ:].reshape(NSEQ, SLEN, DM),
           conv_p[..., :512], p_ssd, p_ret, p_gla, conv_p[..., 512:], lru[:, 0:1],
           conv_s[..., :512], s_ssd, s_ret, s_gla, conv_s[..., 512:], lru[:, 1:])
    return tuple(np.ascontiguousarray(o) for o in out)
```
